# Optimizing a Trainium2 kernel written in Bass

```python
import math
import jax, jax.numpy as jnp
from jax import lax
import numpy as np

D_MODEL = 1024
BATCH = 1
SEQ = 128
DEPTH = 1
DEC_BATCH = 1
DEC_SEQ = 512
PAST_LEN = 256

GRID_W = 64
D_MIX = D_MODEL
ML_WIDTH = D_MIX // 2
ML_HEADS = 4
ML_HEAD_DIM = ML_WIDTH // ML_HEADS
ML_CHUNK = 64
HY_WIDTH = D_MIX - ML_WIDTH
HY_ORDER = 2
HY_SHORT_K = 3
HY_EMB = 33
HY_BANDS = (HY_EMB - 1) // 2
HY_FILTER_HIDDEN = 64
HY_MOD_SHIFT = 0.05
N_GROUPS = 4
EXPERTS_PER_GROUP = 4
N_EXPERTS = N_GROUPS * EXPERTS_PER_GROUP
EXPERT_FF = 512
TOP_K_FINE = 2
N_MOD = 6
EPS = 1e-6
ML_QKVO_COLS = 4 * ML_WIDTH
ML_GATE_COLS = 4 * ML_HEADS
HY_COLS = (HY_ORDER + 1) * HY_WIDTH
IN_COLS = ML_QKVO_COLS + ML_GATE_COLS + HY_COLS

kernel_name = "hymba_mlstm_hyena_hmoe_diffusion_step"

def rms_norm(x, g):
    xf = x.astype(jnp.float32)
    y = xf * lax.rsqrt(jnp.mean(xf * xf, axis=-1, keepdims=True) + EPS)
    return (y * g.astype(jnp.float32)).astype(x.dtype)

def ada_mod(cvec, w_ada, b_ada):
    m = jax.nn.silu(cvec) @ w_ada + b_ada
    return [a[:, None, :] for a in jnp.split(m, N_MOD, axis=-1)]

def _mlstm_chunk(carry, xs):
    m_mat0, n0, m0 = carry
    q, k, v, ig, lf = xs
    ch = q.shape[2]
    b = jnp.cumsum(lf, axis=-1)
    lower = jnp.tril(jnp.ones((ch, ch), dtype=bool))
    logd = jnp.where(lower, b[..., :, None] - b[..., None, :] + ig[..., None, :], -jnp.inf)
    inter = b + m0[..., None]
    m = jnp.maximum(inter, jnp.max(logd, axis=-1))
    s = jnp.einsum('bhjd,bhsd->bhjs', q, k) * jnp.exp(logd - m[..., None])
    sc_inter = jnp.exp(inter - m)
    num = sc_inter[..., None] * jnp.einsum('bhjd,bhde->bhje', q, m_mat0) + jnp.einsum('bhjs,bhse->bhje', s, v)
    den = sc_inter * jnp.einsum('bhjd,bhd->bhj', q, n0) + jnp.sum(s, axis=-1)
    h = num / jnp.maximum(jnp.abs(den), jnp.exp(-m))[..., None]
    b_last = b[..., -1]
    logw = b_last[..., None] - b + ig
    m_new = jnp.maximum(b_last + m0, jnp.max(logw, axis=-1))
    w = jnp.exp(logw - m_new[..., None])
    decay = jnp.exp(b_last + m0 - m_new)
    m_mat = decay[..., None, None] * m_mat0 + jnp.einsum('bhs,bhsd,bhse->bhde', w, k, v)
    n_new = decay[..., None] * n0 + jnp.einsum('bhs,bhsd->bhd', w, k)
    return (m_mat, n_new, m_new), h

def mlstm_scan(q, k, v, ig, lf, state):
    bsz, nh, seq_len, _ = q.shape
    nc = seq_len // ML_CHUNK

    def chunks(a):
        a = a.reshape(a.shape[:2] + (nc, ML_CHUNK) + a.shape[3:])
        return jnp.moveaxis(a, 2, 0)

    st, h = lax.scan(_mlstm_chunk, state, (chunks(q), chunks(k), chunks(v), chunks(ig), chunks(lf)))
    h = jnp.moveaxis(h, 0, 2).reshape(bsz, nh, seq_len, -1)
    return h, st

def short_conv(u, w, grid):
    bsz, seq_len, ch = u.shape
    pad = HY_SHORT_K // 2
    if grid:
        rows = seq_len // GRID_W
        p = jnp.pad(u.reshape(bsz, rows, GRID_W, ch), ((0, 0), (0, 0), (pad, pad), (0, 0)))
        out = sum(w[j] * p[:, :, j:j + GRID_W] for j in range(HY_SHORT_K))
        return out.reshape(bsz, seq_len, ch)
    p = jnp.pad(u, ((0, 0), (pad, pad), (0, 0)))
    return sum(w[j] * p[:, j:j + seq_len] for j in range(HY_SHORT_K))

def hyena_filters(seq_len, p):
    f32 = jnp.float32
    t = jnp.linspace(0.0, 1.0, seq_len, dtype=f32)[:, None]
    wpos = 2.0 * math.pi * jnp.arange(seq_len, dtype=f32)[:, None] / seq_len
    bands = jnp.linspace(1e-4, HY_BANDS - 1, HY_BANDS, dtype=f32)[None, :]
    z = jnp.concatenate([t, jnp.cos(bands * wpos), -jnp.sin(bands * wpos)], axis=-1)
    h = jnp.sin(z @ p['hy_f_w1'].astype(f32) + p['hy_f_b1'].astype(f32))
    h = jnp.sin(h @ p['hy_f_w2'].astype(f32) + p['hy_f_b2'].astype(f32))
    h = (h @ p['hy_f_w3'].astype(f32) + p['hy_f_b3'].astype(f32)).reshape(seq_len, HY_ORDER, 2, HY_WIDTH)
    window = jnp.exp(-t[:, :, None, None] * jnp.abs(p['hy_decay'].astype(f32))) + HY_MOD_SHIFT
    h = h * window
    h = h * lax.rsqrt(jnp.sum(h * h, axis=(0, 2), keepdims=True) + EPS)
    return jnp.transpose(h, (1, 2, 0, 3))

def long_conv(u, h_pos, h_neg, bias):
    seq_len, ch = h_pos.shape
    filt_2l = jnp.concatenate([h_pos[:1] + h_neg[:1], h_pos[1:], jnp.zeros((1, ch), h_pos.dtype), h_neg[:0:-1]], axis=0)
    uf = u.astype(jnp.float32)
    y = jnp.fft.irfft(jnp.fft.rfft(uf, n=2 * seq_len, axis=1) * jnp.fft.rfft(filt_2l, axis=0)[None],
                      n=2 * seq_len, axis=1)[:, :seq_len]
    return (y + bias.astype(jnp.float32) * uf).astype(u.dtype)

def mixer(xm, p, state, grid):
    bsz, seq_len, _ = xm.shape
    f32 = jnp.float32
    proj = xm @ p['w_in']
    q, k, v, o = [proj[..., i * ML_WIDTH:(i + 1) * ML_WIDTH] for i in range(4)]
    gate_pre = proj[..., ML_QKVO_COLS:ML_QKVO_COLS + ML_GATE_COLS]
    hy_in = proj[..., ML_QKVO_COLS + ML_GATE_COLS:]

    def heads(a):
        return a.reshape(bsz, seq_len, ML_HEADS, ML_HEAD_DIM).transpose(0, 2, 1, 3).astype(f32)
    qh, kh, vh = heads(q), heads(k) * (ML_HEAD_DIM ** -0.5), heads(v)
    g = (gate_pre.reshape(bsz, seq_len, 4, ML_HEADS).astype(f32) + p['ml_gate_bias'].astype(f32)).transpose(0, 2, 3, 1)
    c_st, n_st, m_st = [a.astype(f32) for a in state]
    h_f, (cf, nf, mf) = mlstm_scan(qh, kh, vh, g[:, 0], jax.nn.log_sigmoid(g[:, 1]), (c_st[:, 0], n_st[:, 0], m_st[:, 0]))
    rev = lambda a: jnp.flip(a, axis=2)
    h_b, (cb, nb, mb) = mlstm_scan(rev(qh), rev(kh), rev(vh), rev(g[:, 2]), rev(jax.nn.log_sigmoid(g[:, 3])),
                                   (c_st[:, 1], n_st[:, 1], m_st[:, 1]))
    h = h_f + rev(h_b)
    h = h * lax.rsqrt(jnp.mean(h * h, axis=-1, keepdims=True) + EPS)
    y_ml = (h.transpose(0, 2, 1, 3).reshape(bsz, seq_len, ML_WIDTH) * p['ml_head_gain'].astype(f32)
            * jax.nn.sigmoid(o.astype(f32))).astype(xm.dtype)
    new_state = (jnp.stack([cf, cb], axis=1), jnp.stack([nf, nb], axis=1), jnp.stack([mf, mb], axis=1))

    u = short_conv(hy_in, p['hy_conv_w'], grid)
    parts = jnp.split(u, HY_ORDER + 1, axis=-1)
    filt = hyena_filters(seq_len, p)
    z = parts[-1]
    for n in range(HY_ORDER):
        z = parts[n] * long_conv(z, filt[n, 0], filt[n, 1], p['hy_bias'][n])

    y = jnp.concatenate([y_ml, z], axis=-1) @ p['w_out']
    return y, new_state

def hier_moe(x, p):
    bsz, seq_len, d = x.shape
    t = bsz * seq_len
    xt = x.reshape(t, d)
    p_coarse = jax.nn.softmax((xt @ p['w_rc'] + p['b_rc']).astype(jnp.float32), axis=-1)
    p_grp, g_idx = lax.top_k(p_coarse, 1)
    l_fine = (xt @ p['w_rf'] + p['b_rf']).astype(jnp.float32).reshape(t, N_GROUPS, EXPERTS_PER_GROUP)
    l_sel = jnp.take_along_axis(l_fine, g_idx[:, :, None], axis=1)[:, 0]
    top_l, e_idx = lax.top_k(l_sel, TOP_K_FINE)
    w_sel = jax.nn.softmax(top_l, axis=-1) * p_grp
    expert_ids = g_idx * EXPERTS_PER_GROUP + e_idx
    gates = jnp.sum(jax.nn.one_hot(expert_ids, N_EXPERTS, dtype=jnp.float32) * w_sel[..., None], axis=1)
    hg = jnp.einsum('td,edf->tef', xt, p['w_gate'])
    hu = jnp.einsum('td,edf->tef', xt, p['w_up'])
    act = jax.nn.silu(hg) * hu * gates[:, :, None].astype(x.dtype)
    return jnp.einsum('tef,efd->td', act, p['w_down']).reshape(bsz, seq_len, d)

def trunk_layer(x, cvec, p, state, grid):
    sh1, sc1, g1, sh2, sc2, g2 = ada_mod(cvec, p['w_ada'], p['b_ada'])
    h = rms_norm(x, p['g_norm'][0]) * (1.0 + sc1) + sh1
    y, new_state = mixer(h, p, state, grid)
    x = x + g1 * rms_norm(y, p['g_norm'][1])
    h = rms_norm(x, p['g_norm'][2]) * (1.0 + sc2) + sh2
    x = x + g2 * rms_norm(hier_moe(h, p), p['g_norm'][3])
    return x, new_state

def setup_inputs(seed: int = 0) -> dict:
    key = jax.random.key(seed)
    ks = jax.random.split(key, 32)
    nrm = lambda k, s, sc: jax.random.normal(k, s, jnp.float32) * sc
    fg = jnp.linspace(3.0, 6.0, ML_HEADS, dtype=jnp.float32)
    gate_bias = jnp.stack([jnp.zeros((ML_HEADS,)), fg, jnp.zeros((ML_HEADS,)), fg], axis=0)[None]
    decay_base = jnp.linspace(-math.log(1e-2) / 1.5, -math.log(1e-2) / 0.3, HY_WIDTH, dtype=jnp.float32)
    return {
        'x_prompt': nrm(ks[0], (BATCH, SEQ, D_MODEL), 1.0),
        'x_sample': nrm(ks[1], (DEC_BATCH, DEC_SEQ, D_MODEL), 1.0),
        'state_C': nrm(ks[2], (DEC_BATCH, DEPTH, 2, ML_HEADS, ML_HEAD_DIM, ML_HEAD_DIM), 0.05),
        'state_n': nrm(ks[3], (DEC_BATCH, DEPTH, 2, ML_HEADS, ML_HEAD_DIM), 0.1),
        'state_m': nrm(ks[4], (DEC_BATCH, DEPTH, 2, ML_HEADS), 0.5),
        'c': nrm(ks[5], (DEC_BATCH, D_MODEL), 1.0),
        'c_ctx': nrm(ks[6], (D_MODEL,), 1.0),
        'w_ada': nrm(ks[7], (DEPTH, D_MODEL, N_MOD * D_MODEL), 0.5 * D_MODEL ** -0.5),
        'b_ada': nrm(ks[8], (DEPTH, N_MOD * D_MODEL), 0.01),
        'g_norm': 1.0 + nrm(ks[9], (DEPTH, 4, D_MODEL), 0.05),
        'w_in': nrm(ks[10], (DEPTH, D_MODEL, IN_COLS), D_MODEL ** -0.5),
        'ml_gate_bias': gate_bias + nrm(ks[11], (DEPTH, 4, ML_HEADS), 0.1),
        'ml_head_gain': 1.0 + nrm(ks[12], (DEPTH, ML_WIDTH), 0.05),
        'hy_conv_w': nrm(ks[13], (DEPTH, HY_SHORT_K, HY_COLS), 0.5),
        'hy_f_w1': nrm(ks[14], (DEPTH, HY_EMB, HY_FILTER_HIDDEN), HY_EMB ** -0.5),
        'hy_f_b1': nrm(ks[15], (DEPTH, HY_FILTER_HIDDEN), 0.1),
        'hy_f_w2': nrm(ks[16], (DEPTH, HY_FILTER_HIDDEN, HY_FILTER_HIDDEN), HY_FILTER_HIDDEN ** -0.5),
        'hy_f_b2': nrm(ks[17], (DEPTH, HY_FILTER_HIDDEN), 0.1),
        'hy_f_w3': nrm(ks[18], (DEPTH, HY_FILTER_HIDDEN, HY_ORDER * 2 * HY_WIDTH), HY_FILTER_HIDDEN ** -0.5),
        'hy_f_b3': nrm(ks[19], (DEPTH, HY_ORDER * 2 * HY_WIDTH), 0.1),
        'hy_decay': decay_base * (1.0 + nrm(ks[20], (DEPTH, HY_ORDER, 2, HY_WIDTH), 0.05)),
        'hy_bias': nrm(ks[21], (DEPTH, HY_ORDER, HY_WIDTH), 0.5),
        'w_out': nrm(ks[22], (DEPTH, D_MIX, D_MODEL), D_MIX ** -0.5),
        'w_rc': nrm(ks[23], (DEPTH, D_MODEL, N_GROUPS), D_MODEL ** -0.5),
        'b_rc': nrm(ks[24], (DEPTH, N_GROUPS), 0.01),
        'w_rf': nrm(ks[25], (DEPTH, D_MODEL, N_EXPERTS), D_MODEL ** -0.5),
        'b_rf': nrm(ks[26], (DEPTH, N_EXPERTS), 0.01),
        'w_gate': nrm(ks[27], (DEPTH, N_EXPERTS, D_MODEL, EXPERT_FF), D_MODEL ** -0.5),
        'w_up': nrm(ks[28], (DEPTH, N_EXPERTS, D_MODEL, EXPERT_FF), D_MODEL ** -0.5),
        'w_down': nrm(ks[29], (DEPTH, N_EXPERTS, EXPERT_FF, D_MODEL), EXPERT_FF ** -0.5),
    }

def reference(x_prompt, x_sample, state_C, state_n, state_m, c, c_ctx, w_ada, b_ada, g_norm, w_in,
              ml_gate_bias, ml_head_gain, hy_conv_w, hy_f_w1, hy_f_b1, hy_f_w2, hy_f_b2, hy_f_w3, hy_f_b3,
              hy_decay, hy_bias, w_out, w_rc, b_rc, w_rf, b_rf, w_gate, w_up, w_down):
    bsz = x_prompt.shape[0]
    y_p, y_s = x_prompt, x_sample
    new_c, new_n, new_m = [], [], []
    for l in range(DEPTH):
        p = {'w_ada': w_ada[l], 'b_ada': b_ada[l], 'g_norm': g_norm[l], 'w_in': w_in[l],
             'ml_gate_bias': ml_gate_bias[l], 'ml_head_gain': ml_head_gain[l], 'hy_conv_w': hy_conv_w[l],
             'hy_f_w1': hy_f_w1[l], 'hy_f_b1': hy_f_b1[l], 'hy_f_w2': hy_f_w2[l], 'hy_f_b2': hy_f_b2[l],
             'hy_f_w3': hy_f_w3[l], 'hy_f_b3': hy_f_b3[l], 'hy_decay': hy_decay[l], 'hy_bias': hy_bias[l],
             'w_out': w_out[l], 'w_rc': w_rc[l], 'b_rc': b_rc[l], 'w_rf': w_rf[l], 'b_rf': b_rf[l],
             'w_gate': w_gate[l], 'w_up': w_up[l], 'w_down': w_down[l]}
        st0 = (jnp.zeros((bsz, 2, ML_HEADS, ML_HEAD_DIM, ML_HEAD_DIM), jnp.float32),
               jnp.zeros((bsz, 2, ML_HEADS, ML_HEAD_DIM), jnp.float32),
               jnp.zeros((bsz, 2, ML_HEADS), jnp.float32))
        y_p, st = trunk_layer(y_p, c_ctx[None, :], p, st0, grid=False)
        new_c.append(st[0]); new_n.append(st[1]); new_m.append(st[2])
        y_s, _ = trunk_layer(y_s, c, p, (state_C[:, l], state_n[:, l], state_m[:, l]), grid=True)
    new_state_C = jnp.stack(new_c, axis=1)
    new_state_n = jnp.stack(new_n, axis=1)
    new_state_m = jnp.stack(new_m, axis=1)
    return (y_p, y_s, new_state_C, new_state_n, new_state_m)


_drawn_inputs = setup_inputs


def setup_inputs(seed=0):
    import zlib

    import numpy as np

    out = dict(_drawn_inputs(seed))
    spreads = {}
    factors = {'state_C': 3.948, 'state_n': 4.475, 'state_m': 3.164, 'b_rf': 2.727}
    for name, (base, spread) in spreads.items():
        noise = np.random.default_rng([zlib.crc32(name.encode()), seed]).standard_normal(out[name].shape)
        drawn = base * np.exp(spread * noise) if base else spread * noise
        out[name] = __import__('jax').numpy.asarray(drawn.astype(out[name].dtype))
    for name, factor in factors.items():
        out[name] = (out[name] * factor).astype(out[name].dtype)
    return out
```

```python
from contextlib import ExitStack

import numpy as np

import concourse.bass as bass
from concourse import mybir

F32 = mybir.dt.float32
I32 = mybir.dt.int32
ALU = mybir.AluOpType
ACT = mybir.ActivationFunctionType
AX_X = mybir.AxisListType.X

P = 128
D = 1024
KD = D // P
CTX, LAT = 128, 512
TOK = CTX + LAT
NT = TOK // P
LT = LAT // P
H, DH = 4, 128
MW = H * DH
NB = MW // P
CH = 512
GATE0 = 4 * MW
HY0 = GATE0 + 4 * H
ORD = 2
FE, FH = 33, 64
GRID = 64
NG, NE, EPG = 4, 16, 4
FF = 512
UNITS = 2 * H
ROWS = 36
MAXT = NT
TILES = (2 * TOK + NE * (P - 1)) // P
EPS = 1e-6
SHIFT = 0.05
BIG = 1e30
MAGIC = 12582912.0
TWO_PI_HI = 6.28125
TWO_PI_LO = float(2 * np.pi - 6.28125)
PI = 3.1415925


def shape_constants():
    out = {}
    for name, n in (("l", LAT), ("c", CTX)):
        t = np.arange(n)
        ang = np.pi * ((t[:, None] * t[None, :]) % (2 * n)) / n
        sin = np.sin(ang)
        sin[:, 0] = 1.0 - 2.0 * (t % 2)
        out["dft_cos_" + name] = np.cos(ang)
        out["dft_sin_" + name] = sin
        out["dft_sin_t_" + name] = sin.T
    feats, pos = [], []
    bands = np.linspace(1e-4, (FE - 1) // 2 - 1, (FE - 1) // 2, dtype=np.float32)[None, :]
    for n in (CTX, LAT):
        t = np.linspace(0.0, 1.0, n, dtype=np.float32)[:, None]
        w = (2.0 * np.pi * np.arange(n, dtype=np.float32)[:, None] / n).astype(np.float32)
        feats.append(np.concatenate([t, np.cos(bands * w), -np.sin(bands * w)], axis=1))
        pos.append(t[:, 0])
    out["features"] = np.concatenate(feats, axis=0).T
    cols = np.zeros((P, 8))
    cols[:, 0:NT] = np.concatenate(pos).reshape(NT, P).T
    cols[:, 5] = 2.0 / (2 * LAT)
    cols[:, 6] = 2.0 / (2 * CTX)
    cols[0, 5] = 1.0 / (2 * LAT)
    cols[0, 6] = 1.0 / (2 * CTX)
    out["columns"] = cols
    out["ident"] = np.eye(P)
    i = np.arange(P)
    late = np.zeros((P, 4 * P + UNITS * P))
    late[:, 0:P] = np.where(i[:, None] <= i[None, :], 0.0, -BIG)
    late[:, P:2 * P] = np.where(i[:, None] >= i[None, :], 0.0, -BIG)
    late[:, 2 * P:3 * P] = i[:, None] < i[None, :]
    late[:, 3 * P:4 * P] = i[None, :]
    for u in range(UNITS):
        late[32 * (u // H) + u % H, (4 + u) * P:(5 + u) * P] = 1.0
    out["late"] = late
    small = np.zeros((P, 64 + NT))
    small[:, 0:4] = [4, 3, 2, 1]
    small[:, 4:20] = 16 - np.arange(16)
    small[:, 20:25] = np.arange(5)
    small[:, 64:64 + NT] = np.arange(NT)[None, :] * P + i[:, None]
    out["routing"] = small
    return {k: np.ascontiguousarray(v.astype(np.float32)) for k, v in out.items()}


CONST_NAMES = ["dft_cos_l", "dft_sin_l", "dft_sin_t_l", "dft_cos_c", "dft_sin_c", "dft_sin_t_c", "features",
               "columns", "ident", "late", "routing"]


def build(nc, a):
    with ExitStack() as stack:
        emit(nc, a, stack)


def emit(nc, a, stack):
    def sem(name):
        return stack.enter_context(nc.semaphore(name))

    WORDS = 53200
    mem = stack.enter_context(nc.sbuf_tensor("arena", [P, WORDS], F32))
    ps = stack.enter_context(nc.psum_tensor("banks", [P, 8, 512], F32))

    def area(at, *shape, rows=P):
        n = int(np.prod(shape))
        ap = mem[0:rows, at:at + n]
        if len(shape) == 1:
            return ap
        names = "abcd"[:len(shape)]
        return ap.rearrange("p (" + " ".join(names) + ") -> p " + " ".join(names),
                            **{x: s for x, s in zip(names, shape)})

    SLOT = KD * CH
    slot = [area(i * SLOT, KD, CH) for i in range(6)]
    down_slot = [area(i * SLOT, FF // P, D) for i in range(6)]
    W0 = 3 * SLOT
    cos_l = area(W0, LT, LAT)
    sin_l = area(W0 + 2048, LT, LAT)
    sint_l = area(W0 + 4096, LT, LAT)
    cos_c = area(W0 + 6144, CTX)
    sin_c = area(W0 + 6272, CTX)
    sint_c = area(W0 + 6400, CTX)
    W1 = W0 + 6528
    spec_h = area(W1, ORD, 2, NT, MW)
    W2 = W1 + 10240
    part0 = area(W2, NT, MW)
    part2 = area(W2 + 2560, NT, MW)
    part1t = area(W2 + 5120, NB, TOK)
    W3 = W2 + 7680
    hT = area(W3, KD, TOK)
    num = area(W3, NT, UNITS, DH + 1)
    W4 = W3 + 5160
    spec_x = area(W4, 2, LT, MW)
    prod = area(W4 + 4096, 4, MW)
    W5 = W4 + 6144
    ubuf = area(W5, 2, TOK)
    spec_xc = area(W5, 2, MW)
    W6 = W5 + 1280
    assert W6 == 49320
    x_raw = area(W2, NT, D)
    w3e = area(W2 + 5120, 4 * MW, rows=FH + 1)
    sq_l = area(W2 + 7168, MW)
    neg_decay = area(W3, 4 * MW)
    feat = area(W3 + 2048, TOK, rows=FE)
    hid1 = area(W3 + 2688, TOK, rows=FH)
    hid2 = area(W3 + 3328, TOK, rows=FH + 1)
    window = area(W3 + 3968, 2, MW)
    ab = area(W4, 2, NT, MW)
    sqtmp = area(W4 + 5120, 2, MW)
    ytmp = area(W5, TOK, rows=FH)
    qtmp = area(W5 + 640, TOK, rows=FH)
    hy_bias_row = area(W5, ORD, MW, rows=1)
    sq_c = area(W6, MW)
    inv_l = area(W6 + 512, MW)
    inv_c = area(W6 + 1024, MW)
    mask = area(W6, 2, P)
    tri = area(W6 + 256, P)
    iota_row = area(W6 + 384, P)
    sel = area(W6 + 512, UNITS, P, rows=ROWS)
    at = W6 + 1536
    sizes = {}

    def small(n, rows=P, shape=None):
        nonlocal at
        ap = area(at, *(shape or (n,)), rows=rows)
        at += n
        assert at <= WORDS
        return ap

    ident = small(128)
    ones = small(128)
    consts = small(8)
    rows1 = small(128, rows=120)
    rows2 = small(128, rows=16)
    colsT = small(120)
    cvec = small(16, shape=(2, KD))
    mod = small(96, shape=(48, 2))
    scaleA = small(16, shape=(KD, 2))
    pack = small(64, shape=(4, 2, KD))
    b1col = small(2, rows=FH)
    w1sb = small(64, rows=FE)
    w2sb = small(64, rows=FH)
    xss = small(5)
    xrs = small(5)
    gpad = small(5 * 2 * ROWS, shape=(NT, 2, ROWS))
    gbias = small(2, rows=ROWS)
    m0 = small(1, rows=ROWS)
    mprev = small(5, rows=ROWS)
    mend = small(5, rows=ROWS)
    dec = small(5, rows=ROWS)
    mnew = small(2, rows=ROWS)
    epsc = small(1)
    decb = small(40, shape=(UNITS, NT))
    st1 = small(96)
    rconst = small(64 + NT)
    rbias = small(20)
    wrt = small(160, shape=(KD, 20))
    packT = small(128, rows=64)
    stateT = small(8)
    assert at <= WORDS, at
    qT = area(W1, H, TOK)
    kT = area(W1 + 2560, H, TOK)
    W1b = W1 + 5120
    ebuf = area(W1b, H, P)
    wbuf = area(W1b + 512, 2, H, P)
    pbuf = area(W1b + 1536, 2, H, P)
    kw = area(W1b + 2560, 2, H, P)
    qcols = area(W1b + 4096, NT, 4, ROWS)
    v_aug = area(W4, NT, H, DH + 1)
    o_sig = area(W4 + 2580, NT, MW)
    k_tok = area(W2 + 2560, NT, MW)
    c_ctx_st = area(W2, 2, H, DH + 1)
    wgate = area(W2 + 1032, KD, 16)
    c_lat = area(W5, 2, H, DH + 1)
    g_in = area(W0, TOK, rows=ROWS)
    g_f = area(W0 + 640, TOK, rows=ROWS)
    g_t = area(W0 + 1280, TOK, rows=ROWS)
    g_b = area(W0 + 1920, TOK, rows=ROWS)
    g_m = area(W0 + 2560, TOK, rows=ROWS)
    g_nm = area(W0 + 3200, TOK, rows=ROWS)
    g_q = area(W0 + 3840, 4, TOK, rows=ROWS)
    ymlT = area(W1, H, TOK)
    hbuf = area(W0, 2, H, DH)
    htmp = area(W0 + 1024, 2, H, DH)
    tbuf = area(W0 + 2048, D)
    h2buf = area(W0 + 3072, 2, D)
    x2 = area(W2, NT, D)
    row_ctx = [area(W1b + i * 1024, D) for i in range(3)]
    row_lat = [area(W1b + 3072, D), area(W4, D), area(W4 + 1024, D)]
    h2T = area(W4 + 5144, 2, KD, P)
    assert W4 + 5144 + 2048 <= W6
    E0 = W3
    xrows = area(E0, D)
    xT = area(E0 + 1024, KD, P)
    gact = area(E0 + 2048, FF)
    uact = area(E0 + 2560, FF)
    aT = area(E0 + 3072, FF // P, P)
    ysb = area(E0 + 3584, D)
    gr2 = area(E0 + 4608, 2, D)
    R0 = E0 + 6656
    bufr = [R0]

    def rt(*shape):
        n = int(np.prod(shape))
        ap = area(bufr[0], *shape)
        bufr[0] += n
        assert bufr[0] <= W6
        return ap

    rt_e, rt_d, used = rt(NT, NG), rt(NT), rt(NT, NE)
    vhot, phot = rt(2, NT, NE, MAXT), rt(2, NT, P)
    ypair = [area(i * 2048, 2, D) for i in range(NT)]
    fin = [area(NT * 2048 + i * 1024, D) for i in range(NT)]

    row_dram = nc.dram_tensor("modulation_rows", (8, D), F32, kind="Internal").ap()
    h2_dram = nc.dram_tensor("expert_input", (TOK, D), F32, kind="Internal").ap()
    y_dram = nc.dram_tensor("expert_output", (TILES * P, D), F32, kind="Internal").ap()

    names = """ld_ident ld_rows ld_mlp ld_w3 ld_hybias ld_dft ld_x ld_late ld_gate ld_state ld_rowctx ld_rowlat
        ld_x2 ld_route ld_gr2 pack_stored y_zeroed state_stored out_stored y_stored all_stored
        chunk_used setup_t cols_ready cvec_ready mlp_done arg_ready hid_ready ones_ready x_sq x_rstd xn_ready decay_ready
        win_ready filt_done filt_read sq_ready acc_done norm_done norm_sqrt ab_ready modA_ready modB_ready
        xt_done xt_a xt_d hy_done conv_a conv_d tp_done tp_read fw_done fw_read mul_done iv_done iv_read
        pack_t packT_ready qk_done qk_read kt_done kt_read gate_done gate_read gt_done gt_read row_a row_ready m_ready
        qrow_ready qc_done qc_read dec_done vo_done vo_read vones
        bc_done e_ready w_ready s_done p_ready kw_ready inter_done inter_read intra_done num_ready upd_done st_ready
        mstate_t h_ready hsq hss hrs yml_ready yt_done yt_read wo_done wo_sq wo_ss wo_rs x2_sq x2_ss x2_rs h2_ready h2t_done h2t_read
        lg_done rt_v rt_exp pos_done idx_done route_ready
        gather xt_t xT_a xT_d gate_mm silu_ready up_mm act_ready at_t aT_a aT_d down0 down1 y_a y_d
        comb_v comb_sq comb_rs fin_ready act_chain dve_chain pool_chain""".split()
    S = {n: sem(n) for n in names}
    h2_stored = [sem(f"h2_stored{i}") for i in range(2)]
    comb_gather = [sem(f"comb_gather{t}") for t in range(NT)]
    ring_full = [sem(f"ring_full{i}") for i in range(3)]
    w_full = [[sem(f"w_full{h}{i}") for i in range(3)] for h in range(2)]

    w_ada_k = a["w_ada"][0].rearrange("(k p) n -> p k n", p=P)
    w_in_k = a["w_in"][0].rearrange("(k p) n -> p k n", p=P)
    w_out_k = a["w_out"][0].rearrange("(k p) n -> p k n", p=P)
    ada = [w_ada_k[:, :, i * CH:(i + 1) * CH] for i in range(12)]
    hyc = [w_in_k[:, :, HY0 + i * CH:HY0 + (i + 1) * CH] for i in range(3)]
    qkvo = [w_in_k[:, :, i * CH:(i + 1) * CH] for i in range(4)]
    chunks = (ada[0:8] + [hyc[2], ada[8], hyc[0], ada[9], hyc[1], ada[10], ada[11]] + qkvo
              + [w_out_k[:, :, 0:CH], w_out_k[:, :, CH:D]])
    ADA_AT = [0, 1, 2, 3, 4, 5, 6, 7, 9, 11, 13, 14]
    HY_AT, CHUNK_Q, CHUNK_OUT = [8, 10, 12], 15, 19
    NCHUNK = len(chunks)
    xp_t = a["x_prompt"][0]
    xs_t = a["x_sample"][0].rearrange("(t p) d -> p t d", p=P)

    def linker(eng, chain):
        count = {}

        def link(ins, name=chain):
            count[name] = count.get(name, 0) + 1
            ins.then_inc(S[name], 1)
            eng.wait_ge(S[name], count[name])
            return ins
        return link

    def start_at_one(eng, *signals):
        for name in signals:
            eng.sem_inc(S[name], 1)

    tiles_i = area(at + 0, 2 * 17, rows=1).bitcast(I32)
    idx_i = area(at + 34, NE * MAXT).bitcast(I32)
    slot_i = area(at + 114, 2, NT).bitcast(I32)
    idx_now = area(at + 124, 1).bitcast(I32)
    assert at + 125 <= WORDS

    block = stack.enter_context(nc.Block())

    @block.sync
    def _(sp):
        sp.dma_start(ident, a["ident"]).then_inc(S["ld_ident"], 16)
        sp.dma_start(feat, a["features"]).then_inc(S["ld_mlp"], 16)
        sp.dma_start(w1sb, a["hy_f_w1"][0]).then_inc(S["ld_mlp"], 16)
        sp.dma_start(w2sb, a["hy_f_w2"][0]).then_inc(S["ld_mlp"], 16)
        sp.dma_start(b1col[:, 0:1], a["hy_f_b1"][0].rearrange("(n o) -> n o", o=1)).then_inc(S["ld_mlp"], 16)
        sp.dma_start(b1col[:, 1:2], a["hy_f_b2"][0].rearrange("(n o) -> n o", o=1)).then_inc(S["ld_mlp"], 16)
        sp.dma_start(w3e[0:FH, :], a["hy_f_w3"][0]).then_inc(S["ld_w3"], 16)
        sp.dma_start(w3e[FH:FH + 1, :], a["hy_f_b3"]).then_inc(S["ld_w3"], 16)
        sp.dma_start(consts, a["columns"]).then_inc(S["ld_w3"], 16)
        sp.dma_start(neg_decay, a["hy_decay"].rearrange("l o s c -> l (o s c)").broadcast_to((P, 4 * MW)))\
            .then_inc(S["ld_w3"], 16)
        for dst, name in ((cos_l, "dft_cos_l"), (sin_l, "dft_sin_l"), (sint_l, "dft_sin_t_l")):
            sp.dma_start(dst, a[name].rearrange("(b p) f -> p b f", p=P)).then_inc(S["ld_dft"], 16)
        for dst, name in ((cos_c, "dft_cos_c"), (sin_c, "dft_sin_c"), (sint_c, "dft_sin_t_c")):
            sp.dma_start(dst, a[name]).then_inc(S["ld_dft"], 16)
        for n, src in enumerate(chunks):
            if n >= 3:
                sp.wait_ge(S["chunk_used"], n - 2)
            sp.dma_start(slot[n % 3], src).then_inc(ring_full[n % 3], 16)

        def expert(e, half):
            srcs = (a["w_gate"][0, bass.ds(e, 1)].rearrange("o (k p) f -> p (o k) f", p=P),
                    a["w_up"][0, bass.ds(e, 1)].rearrange("o (k p) f -> p (o k) f", p=P),
                    a["w_down"][0, bass.ds(e, 1)].rearrange("o (k p) d -> p (o k) d", p=P))
            for i, src in enumerate(srcs):
                yield (down_slot if i == 2 else slot)[3 * half + i], src, w_full[half][i]

        for i, (dst, src, full) in enumerate(expert(0, 0)):
            sp.wait_ge(S["chunk_used"], NCHUNK - 2 + i)
            sp.dma_start(dst, src).then_inc(full, 16)
        sp.wait_ge(S["h2t_done"], NT)
        sp.wait_ge(h2_stored[0], 16 * 3)
        sp.wait_ge(h2_stored[1], 16 * 2)
        sp.wait_ge(S["chunk_used"], NCHUNK)
        for dst, src, full in expert(1, 1):
            sp.dma_start(dst, src).then_inc(full, 16)
        sp.wait_ge(S["route_ready"], 1)
        with sp.Fori(1, NE // 2) as pair:
            for half in range(2):
                used = sp.value_load(tiles_i[0:1, bass.ds(17 + 2 * pair + half - 1, 1)], min_val=2, max_val=TILES + 1)
                for (dst, src, full), s in zip(expert(2 * pair + half, half), ("gate_mm", "up_mm", "down1")):
                    sp.wait_ge(S[s], used)
                    sp.dma_start(dst, src).then_inc(full, 16)

    @block.gpsimd
    def _(pool):
        link = linker(pool, "pool_chain")
        link(pool.memset(ones, 1.0), "ones_ready")
        link(pool.memset(epsc, EPS), "ones_ready")
        link(pool.memset(hid2[FH:FH + 1, :], 1.0), "ones_ready")
        link(pool.memset(gpad, 0.0), "ones_ready")
        link(pool.memset(gbias, 0.0))
        link(pool.memset(m0, 0.0))
        gb = a["ml_gate_bias"][0].rearrange("g (h o) -> g h o", o=1)
        for r, (i_gate, f_gate) in ((0, (0, 1)), (32, (2, 3))):
            pool.dma_start(gbias[r:r + H, 0:1], gb[i_gate]).then_inc(S["ld_gate"], 16)
            pool.dma_start(gbias[r:r + H, 1:2], gb[f_gate]).then_inc(S["ld_gate"], 16)
            pool.dma_start(m0[r:r + H, :], a["state_m"][0, 0, r // 32].rearrange("(h o) -> h o", o=1))\
                .then_inc(S["ld_gate"], 16)
        pool.dma_start(rconst, a["routing"]).then_inc(S["ld_route"], 16)
        pool.dma_start(rbias[:, 0:4], a["b_rc"].broadcast_to((P, 4))).then_inc(S["ld_route"], 16)
        pool.dma_start(rbias[:, 4:20], a["b_rf"].broadcast_to((P, 16))).then_inc(S["ld_route"], 16)
        pool.dma_start(wrt[:, :, 0:4], a["w_rc"][0].rearrange("(k p) n -> p k n", p=P)).then_inc(S["ld_route"], 16)
        pool.dma_start(wrt[:, :, 4:20], a["w_rf"][0].rearrange("(k p) n -> p k n", p=P)).then_inc(S["ld_route"], 16)
        pool.wait_ge(S["hid_ready"], 2)
        pool.dma_start(hy_bias_row, a["hy_bias"]).then_inc(S["ld_hybias"], 16)
        zero = gpad.rearrange("p t q r -> p (t q r)")[:, 0:P]
        pool.dma_start(y_dram[NE * P:TILES * P, :].rearrange("(p t) (k c) -> p (t k) c", p=P, c=P),
                       zero.unsqueeze(1).broadcast_to((P, (TILES - NE) * KD, P))).then_inc(S["y_zeroed"], 16)
        pool.wait_ge(S["filt_read"], 44)
        pool.dma_start(area(W6, 1536), a["late"]).then_inc(S["ld_late"], 16)
        pool.wait_ge(S["packT_ready"], 1)
        pool.dma_start(row_dram.rearrange("v (k p) -> (v k) p", p=P), packT).then_inc(S["pack_stored"], 16)
        pool.wait_ge(S["iv_read"], 5)
        pool.wait_ge(S["fw_read"], 20)
        pool.dma_start(wgate, w_in_k[:, :, GATE0:GATE0 + 16]).then_inc(S["ld_gate"], 16)
        pool.wait_ge(S["iv_read"], 10)
        pool.dma_start(c_lat[:, :, :, 0:DH], a["state_C"][0, 0].rearrange("r h d e -> d r h e"))\
            .then_inc(S["ld_state"], 16)
        pool.dma_start(c_lat[:, :, :, DH:DH + 1], a["state_n"][0, 0].rearrange("r h (d o) -> d r h o", o=1),
                       allow_slow_non_contiguous=True)\
            .then_inc(S["ld_state"], 16)
        pool.wait_ge(S["st_ready"], 2)
        pool.dma_start(a["out_C"][0, 0].rearrange("r h d e -> d r h e"), c_ctx_st[:, :, :, 0:DH])\
            .then_inc(S["state_stored"], 16)
        pool.dma_start(a["out_n"][0, 0].rearrange("r h (d o) -> d r h o", o=1), c_ctx_st[:, :, :, DH:DH + 1],
                       allow_slow_non_contiguous=True)\
            .then_inc(S["state_stored"], 16)
        for r in (0, 32):
            pool.dma_start(a["out_m"][0, 0, r // 32].rearrange("(h o) -> h o", o=1), mnew[r:r + H, r // 32:r // 32 + 1])\
                .then_inc(S["state_stored"], 16)
        pool.wait_ge(S["num_ready"], 10)
        pool.wait_ge(S["st_ready"], 8)
        pool.wait_ge(S["pack_stored"], 16)
        pool.wait_ge(S["state_stored"], 64)
        for i in range(3):
            pool.dma_start(row_ctx[i], row_dram[2 * i:2 * i + 1, :].broadcast_to((P, D))).then_inc(S["ld_rowctx"], 16)
        pool.dma_start(x2[:, 0, :], xp_t).then_inc(S["ld_x2"], 16)
        for i in range(3):
            pool.dma_start(row_lat[i], row_dram[2 * i + 1:2 * i + 2, :].broadcast_to((P, D)))\
                .then_inc(S["ld_rowlat"], 16)
        pool.dma_start(x2[:, 1:NT, :], xs_t).then_inc(S["ld_x2"], 16)
        pool.wait_ge(h2_stored[0], 16 * 3)
        pool.wait_ge(h2_stored[1], 16 * 2)
        pool.wait_ge(S["route_ready"], 1)
        for g in range(2):
            pool.dma_start(gr2[:, g, :], row_dram[6 + g:7 + g, :].broadcast_to((P, D))).then_inc(S["ld_gr2"], 16)

        def gather_tile(i, col):
            pool.wait_ge(S["xt_t"], i)
            pool.tensor_copy(idx_now, idx_i[:, bass.ds(col, 1)])
            pool.drain()
            pool.indirect_dma_start(xrows, None, h2_dram, bass.IndirectOffsetOnAxis(ap=idx_now, axis=0))\
                .then_inc(S["gather"], 16)

        with pool.Fori(0, NE) as e:
            nt = pool.value_load(tiles_i[0:1, bass.ds(e, 1)], min_val=1, max_val=MAXT)
            first = pool.value_load(tiles_i[0:1, bass.ds(17 + e, 1)], min_val=1, max_val=TILES)
            with pool.Fori(0, nt) as j:
                gather_tile(first + j, e * MAXT + j)
        total = pool.value_load(tiles_i[0:1, 33:34], min_val=NE + 1, max_val=TILES + 1)
        gather_tile(total, total)

        pool.wait_ge(S["all_stored"], 1)
        for t in range(NT):
            for c in range(2):
                pool.indirect_dma_start(ypair[t][:, c, :], None, y_dram,
                                        bass.IndirectOffsetOnAxis(ap=slot_i[:, c, t:t + 1], axis=0))\
                    .then_inc(comb_gather[t], 16)
        for t in range(NT):
            pool.wait_ge(S["fin_ready"], t + 1)
            dst = a["out_p"][0] if t == 0 else a["out_s"][0, (t - 1) * P:t * P, :]
            pool.dma_start(dst, fin[t]).then_inc(S["out_stored"], 16)
        pool.wait_ge(S["out_stored"], 16 * NT)

    steps = [(0, 0), (1, 0)] + [s for k in range(LT) for s in ((0, 1 + k), (1, LT - k))]
    NSTEP = len(steps)
    LAST_UPD = NSTEP - 2

    def half4(h):
        return h // 2, (h % 2) * (DH + 1)

    @block.scalar
    def _(act):
        link = linker(act, "act_chain")
        A = act.activation

        for row, n, src in ((0, 48, a["b_ada"].rearrange("l (k p) -> (l k) p", p=P)),
                            (48, 32, a["g_norm"][0].rearrange("g (k p) -> (g k) p", p=P)),
                            (80, 36, a["hy_conv_w"][0].rearrange("j (k p) -> (j k) p", p=P)),
                            (116, 4, a["ml_head_gain"].rearrange("l (k p) -> (l k) p", p=P))):
            act.dma_start(rows1[row:row + n, :], src).then_inc(S["ld_rows"], 16)
        act.dma_start(rows2[0:KD, :], a["c_ctx"].rearrange("(k p) -> k p", p=P)).then_inc(S["ld_rows"], 16)
        act.dma_start(rows2[KD:2 * KD, :], a["c"].rearrange("l (k p) -> (l k) p", p=P)).then_inc(S["ld_rows"], 16)
        act.dma_start(x_raw[:, 0, :], xp_t).then_inc(S["ld_x"], 16)
        act.dma_start(x_raw[:, 1:NT, :], xs_t).then_inc(S["ld_x"], 16)

        act.wait_ge(S["setup_t"], 2)
        link(A(cvec.rearrange("p g k -> p (g k)"), ps[:, 7, 0:16], ACT.Silu), "cvec_ready")
        for layer in range(2):
            act.wait_ge(S["arg_ready"], layer + 1)
            link(A((hid1, hid2)[layer][0:FH, :], ytmp, ACT.Sin), "hid_ready")
        act.wait_ge(S["ld_x"], 32)
        act.wait_ge(S["ones_ready"], 4)
        junk = area(W1 + 5120, D)
        for t in range(NT):
            link(A(junk, x_raw[:, t, :], ACT.Square, accum_out=xss[:, t:t + 1]), "x_sq")
        link(A(xss, xss, ACT.Sqrt, bias=epsc, scale=1.0 / D), "x_rstd")

        act.wait_ge(S["decay_ready"], 1)

        def win(w):
            o, t, s = w // 10, (w % 10) // 2, w % 2
            if w >= 2:
                act.wait_ge(S["filt_read"], 22 * ((w - 2) // 10) + (w - 2) % 10 + 1)
            c = (2 * o + s) * MW
            link(A(window[:, w % 2, :], neg_decay[:, c:c + MW], ACT.Exp, scale=consts[:, t:t + 1]), "win_ready")

        win(0)
        for w in range(20):
            o, t, s = w // 10, (w % 10) // 2, w % 2
            if w % 10 != 9:
                win(w + 1)
            act.wait_ge(S["filt_read"], 22 * o + w % 10 + 1)
            if w >= 2:
                act.wait_ge(S["acc_done"], w - 1)
            link(A(sqtmp[:, w % 2, :], ab[:, s, t, :], ACT.Square), "sq_ready")
            if w % 10 == 9:
                act.wait_ge(S["norm_done"], o + 1)
                link(A(sq_l, ps[:, 5, :], ACT.Sqrt, bias=epsc))
                link(A(sq_c, ps[:, 6, :], ACT.Sqrt, bias=epsc), "norm_sqrt")
                if o == 0:
                    win(w + 1)

        act.wait_ge(S["modA_ready"], 1)
        for n in range(0, 10, 2):
            act.wait_ge(S["xt_done"], n + 1)
            bank = 1 + n % 4
            if n == 0:
                for k in range(4):
                    link(A(hT[:, k, 0:CTX], ps[:, bank, k * P:(k + 1) * P], ACT.Identity,
                           scale=scaleA[:, k, 0:1], bias=mod[:, k, 0:1]), "xt_a" if k == 3 else "act_chain")
            else:
                k = n - 2
                link(A(hT[:, k, CTX:TOK], ps[:, bank, :], ACT.Identity, scale=scaleA[:, k, 1:2],
                       bias=mod[:, k, 1:2]), "xt_a")

        def taps(n):
            part, blk = ((2, 0, 1)[n // 4], n % 4)
            act.wait_ge(S["hy_done"], n + 1)
            if n >= 2:
                act.wait_ge(S["tp_done"], min(n - 1, 8))
            u = part1t[:, blk, :] if part == 1 else ubuf[:, n % 2, :]
            w = colsT[:, 80 + 12 + part * NB + blk:80 + 13 + part * NB + blk]
            b = 1 + 2 * (n % 2)
            link(A(u[:, CTX:TOK], ps[:, b, :], ACT.Copy, scale=w))
            link(A(u[:, 0:CTX], ps[:, b + 1, 0:CTX], ACT.Copy, scale=w), "conv_a")

        def untranspose(n):
            blk = n % 4
            dst = part2 if n < 4 else part0
            act.wait_ge(S["tp_done"], n + 1)
            link(A(dst[:, 1:NT, blk * P:(blk + 1) * P], ps[:, 5, :].rearrange("p (t c) -> p t c", c=P), ACT.Copy))
            link(A(dst[:, 0, blk * P:(blk + 1) * P], ps[:, 6, 0:P], ACT.Copy), "tp_read")

        for n in range(12):
            taps(n)
            if 1 <= n <= 8:
                untranspose(n - 1)

        def spectra(o):
            for g in range(10):
                act.wait_ge(S["fw_done"], 10 * o + g + 1)
                src = ps[:, 1 + g % 4, :]
                if g < 8:
                    dst, w = spec_x[:, g % 2, g // 2, :], (consts[:, 5:6] if g < 2 else 2.0 / (2 * LAT))
                    if g == 0 and o == 1:
                        act.wait_ge(S["iv_done"], 5)
                else:
                    dst, w = spec_xc[:, g % 2, :], consts[:, 6:7]
                link(A(dst, src, ACT.Copy, scale=w), "fw_read")

        def project_qk(which):
            dst = (qT, kT)[which]
            for n in range(NB):
                act.wait_ge(S["qk_done"], NB * which + n + 1)
                b = 1 + 2 * (n % 2)
                s = DH ** -0.5 if which else 1.0
                link(A(dst[:, n, CTX:TOK], ps[:, b, :], ACT.Copy, scale=s))
                link(A(dst[:, n, 0:CTX], ps[:, b + 1, 0:CTX], ACT.Copy, scale=s), "qk_read")

        spectra(0)
        act.wait_ge(S["modB_ready"], 1)
        act.wait_ge(S["pack_t"], 1)
        link(A(packT, ps[0:64, 0, 0:P], ACT.Copy), "packT_ready")
        act.wait_ge(S["mul_done"], 5)
        project_qk(0)
        spectra(1)
        project_qk(1)
        for t in range(NT):
            act.wait_ge(S["kt_done"], t + 1)
            link(A(k_tok[:, t, :], ps[:, 1 + t % 4, :], ACT.Copy), "kt_read")

        act.wait_ge(S["row_a"], 1)
        link(A(g_t, g_t, ACT.Exp, scale=-1.0))
        link(A(g_t, g_t, ACT.Ln, bias=1.0), "row_ready")

        def values_gates(n):
            act.wait_ge(S["vo_done"], n + 1)
            src = ps[:, 1 + n % 4, :]
            if n < NT:
                link(A(v_aug[:, n, :, 0:DH], src.rearrange("p (h e) -> p h e", h=H), ACT.Copy), "vo_read")
            else:
                link(A(o_sig[:, n - NT, :], src, ACT.Sigmoid), "vo_read")

        for n in range(NT):
            values_gates(n)
        act.wait_ge(S["m_ready"], 1)
        link(A(dec, dec, ACT.Exp), "qrow_ready")
        for n, (t0, t1) in enumerate(((0, 3), (3, 5))):
            act.wait_ge(S["qc_done"], n + 1)
            src = ps[:, 5 + n, 0:(t1 - t0) * 4 * ROWS].rearrange("p (t q r) -> p t q r", q=4, r=ROWS)
            link(A(qcols[:, t0:t1, 0, :], src[:, :, 0, :], ACT.Copy))
            link(A(qcols[:, t0:t1, 1:4, :], src[:, :, 1:4, :], ACT.Exp), "qc_read")
        act.wait_ge(S["dec_done"], 1)
        link(A(decb, ps[:, 7, 0:UNITS * NT].rearrange("p (u t) -> p u t", t=NT), ACT.Copy), "qc_read")

        for n in range(NT, 2 * NT):
            values_gates(n)

        def weights(i):
            d, t = steps[i]
            act.wait_ge(S["e_ready"], i + 1)
            if i >= 2:
                act.wait_ge(S["p_ready"], i - 1)
            for h in range(H):
                link(A(wbuf[:, i % 2, h, :], ebuf[:, h, :], ACT.Exp, bias=qcols[:, t, 0, 32 * d + h:32 * d + h + 1]),
                     "w_ready" if h == 3 else "act_chain")

        weights(0)
        for i in range(NSTEP):
            if i + 1 < NSTEP:
                weights(i + 1)
            d, t = steps[i]
            if t:
                act.wait_ge(S["inter_done"], i - 1)
                for h in range(H):
                    b, c = half4(h)
                    link(A(num[:, t, H * d + h, :], ps[:, 4 + b, c:c + DH + 1], ACT.Copy,
                           scale=qcols[:, t, 1, 32 * d + h:32 * d + h + 1]), "inter_read" if h == 3 else "act_chain")

        def norm_heads(t):
            act.wait_ge(S["h_ready"], t + 1)
            link(A(htmp[:, t % 2], hbuf[:, t % 2], ACT.Square), "hsq")
            act.wait_ge(S["hss"], t + 1)
            link(A(st1[:, 4 * t:4 * t + 4], st1[:, 4 * t:4 * t + 4], ACT.Sqrt, bias=epsc, scale=1.0 / DH), "hrs")

        def residual(t):
            act.wait_ge(S["wo_done"], t + 1)
            b = 1 + 2 * (t % 2)
            for c in range(2):
                link(A(h2buf[:, t % 2, c * CH:(c + 1) * CH], ps[:, b + c, :], ACT.Square,
                       accum_out=st1[:, 20 + 2 * t + c:21 + 2 * t + c]), "wo_sq")
            act.wait_ge(S["wo_ss"], t + 1)
            link(A(st1[:, 30 + t:31 + t], st1[:, 30 + t:31 + t], ACT.Sqrt, bias=epsc, scale=1.0 / D), "wo_rs")
            act.wait_ge(S["x2_sq"], t + 1)
            link(A(h2buf[:, t % 2, :], x2[:, t, :], ACT.Square, accum_out=st1[:, 35 + t:36 + t]))
            link(A(st1[:, 35 + t:36 + t], st1[:, 35 + t:36 + t], ACT.Sqrt, bias=epsc, scale=1.0 / D), "x2_rs")
            act.wait_ge(S["h2_ready"], t + 1)
            act.dma_start(h2_dram[t * P:(t + 1) * P, :], h2buf[:, t % 2, :]).then_inc(h2_stored[t % 2], 16)

        def h2_columns(t):
            act.wait_ge(S["h2t_done"], t + 1)
            if t >= 2:
                act.wait_ge(S["lg_done"], t - 1)
            for c in range(2):
                link(A(h2T[:, t % 2, 4 * c:4 * c + 4, :], ps[:, 5 + c, :].rearrange("p (k t) -> p k t", t=P), ACT.Copy),
                     "h2t_read" if c else "act_chain")

        norm_heads(0)
        for t in range(NT):
            if t + 1 < NT:
                norm_heads(t + 1)
            if t >= 2:
                act.wait_ge(h2_stored[t % 2], 16 * (t // 2))
            residual(t)
            if t:
                h2_columns(t - 1)
        h2_columns(NT - 1)

        act.wait_ge(S["rt_v"], 1)
        link(A(rt_e, rt_e, ACT.Exp))
        link(A(rt_d, rt_d, ACT.Exp), "rt_exp")

        act.wait_ge(S["route_ready"], 1)

        def x_half(i):
            act.wait_ge(S["xt_t"], i + 1)
            act.activation(xT[:, 0:4, :], ps[:, 0, :].rearrange("p (k t) -> p k t", t=P), ACT.Copy)\
                .then_inc(S["xT_a"], 1)

        start_at_one(act, "silu_ready", "xT_a", "aT_a", "y_a")
        act.sem_inc(S["y_stored"], 16)
        x_half(1)
        with act.Fori(0, NE) as e:
            nt = act.value_load(tiles_i[0:1, bass.ds(e, 1)], min_val=1, max_val=MAXT)
            first = act.value_load(tiles_i[0:1, bass.ds(17 + e, 1)], min_val=1, max_val=TILES)
            with act.Fori(0, nt) as j:
                i = first + j
                act.wait_ge(S["gate_mm"], i + 1)
                act.wait_ge(S["act_ready"], i)
                act.activation(gact, ps[:, 2, :], ACT.Silu).then_inc(S["silu_ready"], 1)
                x_half(i + 1)
                act.wait_ge(S["at_t"], i + 1)
                act.activation(aT[:, 0:2, :], ps[:, 4, 0:2 * P].rearrange("p (k t) -> p k t", t=P), ACT.Copy)\
                    .then_inc(S["aT_a"], 1)
                act.wait_ge(S["down0"], i + 1)
                act.wait_ge(S["y_stored"], 16 * i)
                act.activation(ysb[:, 0:CH], ps[:, 5, :], ACT.Copy).then_inc(S["y_a"], 1)
                act.wait_ge(S["y_a"], i + 1)
                act.wait_ge(S["y_d"], i + 1)
                row = nc.s_assert_within(i - 1, 0, TILES - 1, 
                                          skip_runtime_bounds_check_because="at most TILES tiles in all") * P
                act.dma_start(y_dram[bass.ds(row, P), :], ysb).then_inc(S["y_stored"], 16)

        total = act.value_load(tiles_i[0:1, 33:34], min_val=NE + 1, max_val=TILES + 1)
        act.wait_ge(S["y_stored"], 16 * total)
        link(A(st1[:, 70:71], epsc, ACT.Copy), "all_stored")
        for t in range(NT):
            act.wait_ge(S["comb_v"], t + 1)
            link(A(ypair[t][:, 1, :], ypair[t][:, 0, :], ACT.Square, accum_out=st1[:, 60 + t:61 + t]))
            link(A(st1[:, 60 + t:61 + t], st1[:, 60 + t:61 + t], ACT.Sqrt, bias=epsc, scale=1.0 / D), "comb_rs")

    @block.vector
    def _(dve):
        link = linker(dve, "dve_chain")
        TT, TS, STT, CP = dve.tensor_tensor, dve.tensor_scalar, dve.scalar_tensor_tensor, dve.tensor_copy

        dve.wait_ge(S["setup_t"], 1)
        link(CP(colsT, ps[:, 0, 0:120]), "cols_ready")
        for layer in range(2):
            dve.wait_ge(S["mlp_done"], layer + 1)
            b = 1 + 2 * layer
            link(TS(ytmp[:, CTX:TOK], ps[0:FH, b, :], b1col[:, layer:layer + 1], None, ALU.add))
            link(TS(ytmp[:, 0:CTX], ps[0:FH, b + 1, 0:CTX], b1col[:, layer:layer + 1], None, ALU.add))
            link(TS(qtmp, ytmp, 1.0 / (2.0 * np.pi), MAGIC, ALU.mult, ALU.add))
            link(TS(qtmp, qtmp, MAGIC, None, ALU.subtract))
            link(STT(ytmp, qtmp, -TWO_PI_HI, ytmp, ALU.mult, ALU.add))
            link(STT(ytmp, qtmp, -TWO_PI_LO, ytmp, ALU.mult, ALU.add))
            link(TS(ytmp, ytmp, PI, -PI, ALU.min, ALU.max), "arg_ready")
        dve.wait_ge(S["ld_w3"], 64)
        link(STT(neg_decay, neg_decay, -1.0, neg_decay, ALU.mult, ALU.min), "decay_ready")
        dve.wait_ge(S["x_rstd"], 1)
        link(dve.reciprocal(xrs, xss))
        for t in range(NT):
            link(TS(x_raw[:, t, :], x_raw[:, t, :], xrs[:, t:t + 1], None, ALU.mult), "xn_ready")

        def add_square(w):
            t = (w % 10) // 2
            dve.wait_ge(S["sq_ready"], w + 1)
            acc = sq_c if t == 0 else sq_l
            if w % 10 in (0, 2):
                link(CP(acc, sqtmp[:, w % 2, :]), "acc_done")
            else:
                link(TT(acc, acc, sqtmp[:, w % 2, :], ALU.add), "acc_done")

        for o in range(ORD):
            for w in range(10):
                t, s, n = w // 2, w % 2, 22 * o + w
                dve.wait_ge(S["filt_done"], n + 1)
                dve.wait_ge(S["win_ready"], 10 * o + w + 1)
                link(STT(ab[:, s, t, :], window[:, w % 2, :], SHIFT, ps[:, 1 + n % 4, :], ALU.add, ALU.mult),
                     "filt_read")
                if w:
                    add_square(10 * o + w - 1)
            add_square(10 * o + 9)
            link(TT(ab[:, 1], ab[:, 1], ab[:, 0], ALU.subtract))
            link(STT(ab[:, 0], ab[:, 0], 2.0, ab[:, 1], ALU.mult, ALU.add))
            dve.wait_ge(S["norm_sqrt"], o + 1)
            link(dve.reciprocal(inv_l, sq_l))
            link(dve.reciprocal(inv_c, sq_c))
            dve.wait_ge(S["ld_hybias"], 16)
            for norm, t in ((sq_l, 1), (sq_c, 0)):
                link(TT(norm[0:1, :], norm[0:1, :], hy_bias_row[:, o, :], ALU.mult))
                link(TT(ab[0:1, 0, t, :], ab[0:1, 0, t, :], norm[0:1, :], ALU.add),
                     "ab_ready" if t == 0 else "dve_chain")
            for g in range(12):
                n = 22 * o + 10 + g
                dve.wait_ge(S["filt_done"], n + 1)
                src = ps[:, 1 + n % 4, :]
                if g in (2, 11):
                    f, inv = (0, inv_l) if g == 2 else (NT - 1, inv_c)
                    link(TT(spec_h[0:1, o, 1, f, :], src[0:1, :], inv[0:1, :], ALU.mult), "filt_read")
                else:
                    q = g if g < 2 else g - 1
                    f, inv = q // 2, (inv_c if g >= 9 else inv_l)
                    link(TT(spec_h[:, o, q % 2, f, :], src, inv, ALU.mult), "filt_read")

        dve.wait_ge(S["chunk_used"], 4)
        link(TT(mod[:, 0:16, :], ps[:, 0, 0:32].rearrange("p (n g) -> p n g", g=2),
                colsT[:, 0:16].unsqueeze(2).broadcast_to((P, 16, 2)), ALU.add))
        link(STT(scaleA, mod[:, 8:16, :], 1.0, colsT[:, 48:56].unsqueeze(2).broadcast_to((P, 8, 2)),
                 ALU.add, ALU.mult), "modA_ready")
        for n in range(1, 10, 2):
            dve.wait_ge(S["xt_done"], n + 1)
            bank = 1 + n % 4
            if n == 1:
                for k in range(4, 8):
                    link(TS(hT[:, k, 0:CTX], ps[:, bank, (k - 4) * P:(k - 3) * P], scaleA[:, k, 0:1],
                            mod[:, k, 0:1], ALU.mult, ALU.add), "xt_d" if k == 7 else "dve_chain")
            else:
                k = n - 2
                link(TS(hT[:, k, CTX:TOK], ps[:, bank, :], scaleA[:, k, 1:2], mod[:, k, 1:2],
                        ALU.mult, ALU.add), "xt_d")

        for n in range(12):
            part, blk = ((2, 0, 1)[n // 4], n % 4)
            dve.wait_ge(S["conv_a"], n + 1)
            u = part1t[:, blk, :] if part == 1 else ubuf[:, n % 2, :]
            b, c = 1 + 2 * (n % 2), 80 + part * NB + blk
            ul = u[:, CTX:TOK].rearrange("p (r x) -> p r x", x=GRID)
            pl = ps[:, b, :].rearrange("p (r x) -> p r x", x=GRID)
            uc, pc = u[:, 0:CTX], ps[:, b + 1, 0:CTX]
            w0, w2 = colsT[:, c:c + 1], colsT[:, c + 24:c + 25]
            link(STT(ul[:, :, 1:], pl[:, :, :-1], w0, ul[:, :, 1:], ALU.mult, ALU.add))
            link(STT(ul[:, :, :-1], pl[:, :, 1:], w2, ul[:, :, :-1], ALU.mult, ALU.add))
            link(STT(uc[:, 1:], pc[:, :-1], w0, uc[:, 1:], ALU.mult, ALU.add))
            link(STT(uc[:, :-1], pc[:, 1:], w2, uc[:, :-1], ALU.mult, ALU.add), "conv_d")

        def products(o):
            for f in range(NT):
                dve.wait_ge(S["fw_read"], 10 * o + 2 * f + 2)
                xc, xs = (spec_x[:, 0, f, :], spec_x[:, 1, f, :]) if f < LT else (spec_xc[:, 0, :], spec_xc[:, 1, :])
                hc, hs = spec_h[:, o, 0, f, :], spec_h[:, o, 1, f, :]
                p = [prod[:, i, :] for i in range(4)]
                link(TT(p[0], xc, hc, ALU.mult))
                link(TT(p[1], xs, hs, ALU.mult))
                link(TT(p[2], xs, hc, ALU.mult))
                link(TT(p[3], xc, hs, ALU.mult))
                last = f in (0, LT)
                link(TT(xc, p[0], p[1], ALU.add))
                link(TT(xs, p[2], p[3], ALU.subtract), "dve_chain" if last else "mul_done")
                if last:
                    link(CP(xc[0:1, :], p[0][0:1, :]))
                    link(CP(xs[0:1, :], p[1][0:1, :]), "mul_done")

        products(0)
        dve.wait_ge(S["chunk_used"], CHUNK_Q)
        link(TT(mod[:, 16:48, :], ps[:, 7, 32:96].rearrange("p (n g) -> p n g", g=2),
                colsT[:, 16:48].unsqueeze(2).broadcast_to((P, 32, 2)), ALU.add))

        def gain(i):
            return colsT[:, 48 + 8 * i:56 + 8 * i].unsqueeze(1).broadcast_to((P, 2, KD))

        def modv(i):
            return mod[:, 8 * i:8 * i + 8, :].rearrange("p k g -> p g k")

        link(TT(pack[:, 0], modv(2), gain(1), ALU.mult))
        link(STT(pack[:, 1], modv(4), 1.0, gain(2), ALU.add, ALU.mult))
        link(CP(pack[:, 2], modv(3)))
        link(TT(pack[:, 3], modv(5), gain(3), ALU.mult), "modB_ready")

        for t in range(NT):
            tile = t + 1 if t < LT else 0
            dve.wait_ge(S["iv_done"], t + 1)
            link(TT(part0[:, tile, :], part0[:, tile, :], ps[:, 5 + t % 2, :], ALU.mult), "iv_read")
        products(1)
        for n in range(5):
            dve.wait_ge(S["iv_done"], NT + n + 1)
            src = ps[:, 5 + (NT + n) % 2, :]
            if n < NB:
                link(TT(part1t[:, n, CTX:TOK], part1t[:, n, CTX:TOK], src, ALU.mult), "iv_read")
            else:
                link(TT(part1t[:, :, 0:CTX], part1t[:, :, 0:CTX], src.rearrange("p (c t) -> p c t", t=CTX), ALU.mult),
                     "iv_read")

        dve.wait_ge(S["gate_done"], 1)
        dve.wait_ge(S["y_zeroed"], 16)
        gsrc = ps[:, 7, 0:NT * 16].rearrange("p (t g h) -> p t g h", g=4, h=H)
        link(CP(gpad[:, :, :, 0:H], gsrc[:, :, 0:2, :]))
        link(CP(gpad[:, :, :, 32:32 + H], gsrc[:, :, 2:4, :]), "gate_read")
        dve.wait_ge(S["gt_done"], 1)
        for i, dst in enumerate((g_in, g_f)):
            link(TS(dst[:, CTX:TOK], ps[0:ROWS, 5 + i, :], gbias[:, i:i + 1], None, ALU.add))
            link(TS(dst[:, 0:CTX], ps[0:ROWS, 0, i * P:(i + 1) * P], gbias[:, i:i + 1], None, ALU.add),
                 "gt_read" if i else "dve_chain")
        link(STT(g_t, g_f, -1.0, g_f, ALU.mult, ALU.max), "row_a")
        link(dve.memset(g_b, 0.0))
        link(dve.memset(g_m, 0.0))
        link(dve.memset(g_q[:, 0, :], 1.0))
        link(dve.memset(g_q[:, 1, :], 0.0))
        dve.wait_ge(S["row_ready"], 1)
        link(STT(g_f, g_f, 0.0, g_t, ALU.min, ALU.subtract))

        def scans(dst, op0, init_l, init_c, coef, src, op1):
            for r, turn in ((0, 1), (32, -1)):
                for lo, hi, init in ((0, CTX, init_c), (CTX, TOK, init_l)):
                    def cut(x):
                        y = x[r:r + H, lo:hi]
                        return y if turn == 1 else y[:, ::-1]
                    start = init if type(init) is float else init[r:r + H, :]
                    link(dve.tensor_tensor_scan(cut(dst), cut(coef), cut(src), start, op0, op1))

        scans(g_b, ALU.mult, 0.0, 0.0, g_q[:, 0, :], g_f, ALU.add)
        link(TT(g_in, g_in, g_b, ALU.subtract))
        scans(g_m, ALU.add, m0, 0.0, g_q[:, 1, :], g_in, ALU.max)
        link(dve.memset(mprev, 0.0))
        link(dve.memset(mend, 0.0))
        link(CP(mprev[0:H, 1:2], m0[0:H, :]))
        link(CP(mprev[0:H, 2:NT], g_m[0:H, CTX + P - 1:TOK - 1:P]))
        link(CP(mend[0:H, :], g_m[0:H, P - 1:TOK:P]))
        link(CP(mprev[32:ROWS, NT - 1:NT], m0[32:ROWS, :]))
        link(CP(mprev[32:ROWS, 1:NT - 1], g_m[32:ROWS, 2 * P:TOK:P]))
        link(CP(mend[32:ROWS, :], g_m[32:ROWS, 0:TOK:P]))
        link(TS(g_nm, g_m, -1.0, None, ALU.mult))
        tiled = [g_q[:, q, :].rearrange("p (t j) -> p t j", j=P) for q in range(4)]
        link(CP(g_q[:, 0, :], g_in))
        link(TT(tiled[1], g_nm.rearrange("p (t j) -> p t j", j=P), mprev.unsqueeze(2).broadcast_to((ROWS, NT, P)),
                ALU.add))
        link(TT(g_q[:, 2, :], g_nm, g_b, ALU.subtract))
        link(TT(tiled[3], g_in.rearrange("p (t j) -> p t j", j=P), mend.unsqueeze(2).broadcast_to((ROWS, NT, P)),
                ALU.subtract))
        link(TT(mnew[0:H, 0:1], g_b[0:H, CTX - 1:CTX], g_m[0:H, CTX - 1:CTX], ALU.add))
        link(TT(mnew[32:ROWS, 1:2], g_b[32:ROWS, 0:1], g_m[32:ROWS, 0:1], ALU.add))
        link(TT(dec, mprev, mend, ALU.subtract), "m_ready")
        dve.wait_ge(S["fw_read"], 20)
        dve.wait_ge(S["iv_done"], 10)
        link(dve.memset(v_aug[:, :, :, DH:DH + 1], 1.0), "vones")

        def exponents(i):
            d, t = steps[i]
            dve.wait_ge(S["bc_done"], i + 1)
            if i:
                dve.wait_ge(S["w_ready"], i)
            link(TT(ebuf, ps[:, 0, :].rearrange("p (h j) -> p h j", h=H),
                    mask[:, d, :].unsqueeze(1).broadcast_to((P, H, P)), ALU.add), "e_ready")
            if i < LAST_UPD:
                if i >= 2:
                    dve.wait_ge(S["upd_done"], i - 1)
                link(TT(kw[:, i % 2], k_tok[:, t, :].rearrange("p (h d) -> p h d", h=H),
                        qcols[:, t, 3, 32 * d:32 * d + H].unsqueeze(2).broadcast_to((P, H, DH)), ALU.mult), "kw_ready")

        dve.wait_ge(S["ld_late"], 16)
        dve.wait_ge(S["ld_state"], 32)
        dve.wait_ge(S["qc_read"], 3)
        exponents(0)
        for i in range(NSTEP):
            d, t = steps[i]
            dve.wait_ge(S["w_ready"], i + 1)
            dve.wait_ge(S["s_done"], i + 1)
            if i >= 2:
                dve.wait_ge(S["intra_done"], i - 1)
            link(TT(pbuf[:, i % 2], wbuf[:, i % 2], ps[:, 1, :].rearrange("p (h j) -> p h j", h=H), ALU.mult), "p_ready")
            if i + 1 < NSTEP:
                exponents(i + 1)
            dve.wait_ge(S["intra_done"], i + 1)
            out = num[:, t, H * d:H * d + H, :].rearrange("p (b h) e -> p b (h e)", b=2)
            src = ps[:, 2:4, 0:2 * (DH + 1)]
            if t == 0:
                link(CP(out, src), "num_ready")
            else:
                dve.wait_ge(S["inter_read"], i - 1)
                link(TT(out, out, src, ALU.add), "num_ready")
            if i < LAST_UPD:
                dve.wait_ge(S["upd_done"], i + 1)
                upd = ps[:, 6:8, 0:2 * (DH + 1)]
                if t == 0:
                    link(CP(c_ctx_st[:, d].rearrange("p (b h) e -> p b (h e)", b=2), upd), "st_ready")
                else:
                    dve.wait_ge(S["inter_done"], i - 1)
                    for h in range(H):
                        b, c = half4(h)
                        link(STT(c_lat[:, d, h, :], c_lat[:, d, h, :], decb[:, H * d + h, t:t + 1],
                                 ps[:, 6 + b, c:c + DH + 1], ALU.mult, ALU.add), "st_ready" if h == 3 else "dve_chain")

        def mix_heads(t):
            den = num[:, t, :, DH]
            r = st1[:, 44:52]
            link(STT(r, den, -1.0, den, ALU.mult, ALU.max))
            for d in range(2):
                link(TT(r[:, H * d:H * d + H], r[:, H * d:H * d + H], qcols[:, t, 2, 32 * d:32 * d + H], ALU.max))
            link(dve.reciprocal(r, r))
            hb, ht = hbuf[:, t % 2], htmp[:, t % 2]
            if t >= 2:
                dve.wait_ge(S["yt_done"], t - 1)
            link(TT(hb, num[:, t, 0:H, 0:DH], r[:, 0:H].unsqueeze(2).broadcast_to((P, H, DH)), ALU.mult))
            link(TT(ht, num[:, t, H:2 * H, 0:DH], r[:, H:2 * H].unsqueeze(2).broadcast_to((P, H, DH)), ALU.mult))
            link(TT(hb, hb, ht, ALU.add), "h_ready")
            dve.wait_ge(S["hsq"], t + 1)
            s = st1[:, 4 * t:4 * t + 4]
            link(dve.tensor_reduce(s, ht, AX_X, ALU.add), "hss")
            dve.wait_ge(S["hrs"], t + 1)
            link(dve.reciprocal(s, s))
            link(TT(hb, hb, s.unsqueeze(2).broadcast_to((P, H, DH)), ALU.mult))
            link(TT(hb, hb, o_sig[:, t, :].rearrange("p (h e) -> p h e", h=H), ALU.mult), "yml_ready")

        def turn_heads(t):
            dve.wait_ge(S["yt_done"], t + 1)
            link(TT(ymlT[:, :, t * P:(t + 1) * P], ps[:, 0, :].rearrange("p (h t) -> p h t", t=P),
                    colsT[:, 116:120].unsqueeze(2).broadcast_to((P, H, P)), ALU.mult), "yt_read")

        def residual(t):
            rows = row_ctx if t == 0 else row_lat
            if t == 0:
                dve.wait_ge(S["ld_rowctx"], 48)
                dve.wait_ge(S["ld_x2"], 32)
            if t == 1:
                dve.wait_ge(S["ld_rowlat"], 48)
            b = 1 + 2 * (t % 2)
            dve.wait_ge(S["wo_sq"], 2 * t + 2)
            s = st1[:, 30 + t:31 + t]
            link(TT(s, st1[:, 20 + 2 * t:21 + 2 * t], st1[:, 21 + 2 * t:22 + 2 * t], ALU.add), "wo_ss")
            dve.wait_ge(S["wo_rs"], t + 1)
            link(dve.reciprocal(s, s))
            link(STT(tbuf.rearrange("p (b n) -> p b n", b=2), ps[:, b:b + 2, :], s,
                     rows[0].rearrange("p (b n) -> p b n", b=2), ALU.mult, ALU.mult))
            link(TT(x2[:, t, :], x2[:, t, :], tbuf, ALU.add), "x2_sq")
            dve.wait_ge(S["x2_rs"], t + 1)
            s = st1[:, 35 + t:36 + t]
            link(dve.reciprocal(s, s))
            link(STT(tbuf, x2[:, t, :], s, rows[1], ALU.mult, ALU.mult))
            link(TT(h2buf[:, t % 2, :], tbuf, rows[2], ALU.add), "h2_ready")

        mix_heads(0)
        turn_heads(0)
        for t in range(NT):
            if t + 1 < NT:
                mix_heads(t + 1)
                turn_heads(t + 1)
            residual(t)

        dve.wait_ge(S["lg_done"], NT)
        dve.wait_ge(S["ld_route"], 80)
        lg = rt(NT, 20)
        r4, r16, r5 = rconst[:, 0:4], rconst[:, 4:20], rconst[:, 20:25]

        def over(x, *dims):
            return x.broadcast_to((P,) + dims)

        link(TT(lg, ps[:, 7, 0:NT * 20].rearrange("p (t n) -> p t n", n=20), over(rbias.unsqueeze(1), NT, 20), ALU.add))
        coarse = lg[:, :, 0:NG]
        cmax, gmax, top1, top2, pg, rk = (rt(NT) for _ in range(6))
        link(dve.tensor_reduce(cmax, coarse, AX_X, ALU.max))
        link(TT(rt_e, coarse, over(cmax.unsqueeze(2), NT, NG), ALU.subtract))
        g1h = rt(NT, NG)
        link(TT(g1h, coarse, over(cmax.unsqueeze(2), NT, NG), ALU.is_equal))
        link(TT(g1h, g1h, over(r4.unsqueeze(1), NT, NG), ALU.mult))
        link(dve.tensor_reduce(gmax, g1h, AX_X, ALU.max))
        link(TT(g1h, over(r4.unsqueeze(1), NT, NG), over(gmax.unsqueeze(2), NT, NG), ALU.is_equal))
        link(TS(g1h, g1h, BIG, -BIG, ALU.mult, ALU.add))
        fine = rt(NT, NE)
        link(TT(fine.rearrange("p t (g e) -> p t g e", g=NG), lg[:, :, NG:20].rearrange("p t (g e) -> p t g e", g=NG),
                over(g1h.unsqueeze(3), NT, NG, EPG), ALU.add))
        picks = rt(2, NT, NE)
        for c, top in enumerate((top1, top2)):
            e1h = picks[:, c]
            link(dve.tensor_reduce(top, fine, AX_X, ALU.max))
            link(TT(e1h, fine, over(top.unsqueeze(2), NT, NE), ALU.is_equal))
            link(TT(e1h, e1h, over(r16.unsqueeze(1), NT, NE), ALU.mult))
            link(dve.tensor_reduce(rk, e1h, AX_X, ALU.max))
            link(TT(e1h, over(r16.unsqueeze(1), NT, NE), over(rk.unsqueeze(2), NT, NE), ALU.is_equal))
            if c == 0:
                link(STT(fine, e1h, -3.0 * BIG, fine, ALU.mult, ALU.add))
        link(TT(used, picks[:, 0], picks[:, 1], ALU.add))
        link(TT(rt_d, top2, top1, ALU.subtract), "rt_v")
        dve.wait_ge(S["pos_done"], 1)
        pos, tot = rt(NT, NE), rt(NT, NE)
        link(CP(tot, ps[:, 6, 0:NT * NE].rearrange("p (t e) -> p t e", e=NE)))
        link(CP(pos, ps[:, 5, 0:NT * NE].rearrange("p (t e) -> p t e", e=NE)))
        for t in range(1, NT):
            link(TT(pos[:, t, :], pos[:, t, :], tot[:, t - 1, :], ALU.add))
            link(TT(tot[:, t, :], tot[:, t, :], tot[:, t - 1, :], ALU.add))
        cnt, nt_f = tot[:, NT - 1, :], rt(NE)
        link(TS(nt_f, cnt, float(P), 1.0, ALU.is_gt, ALU.add))
        for j in range(2, MAXT):
            link(STT(nt_f, cnt, float(j * P), nt_f, ALU.is_gt, ALU.add))
        cum = rt(NE + 1)
        link(dve.memset(cum, 1.0))
        link(dve.tensor_tensor_scan(cum[:, 1:NE + 1], ones[:, 0:NE], nt_f, 1.0, ALU.mult, ALU.add))
        link(CP(tiles_i[0:1, 0:NE], nt_f[0:1, :]))
        link(CP(tiles_i[0:1, 17:34], cum[0:1, :]))
        ck = rt(2, NT, NE)
        pk, qk, sl = rt(2, NT), rt(2, NT), rt(2, NT)
        jq = rt(2, NT, MAXT)
        link(TT(ck, picks, over(pos.unsqueeze(1), 2, NT, NE), ALU.mult))
        link(dve.tensor_reduce(pk, ck, AX_X, ALU.add))
        link(TT(ck, picks, over(cum[:, 0:NE].unsqueeze(1).unsqueeze(1), 2, NT, NE), ALU.mult))
        link(dve.tensor_reduce(sl, ck, AX_X, ALU.add))
        link(TS(sl, sl, float(P), -float(P), ALU.mult, ALU.add))
        link(TT(sl, sl, pk, ALU.add))
        link(CP(slot_i, sl))
        link(TS(qk, pk, float(P), None, ALU.is_ge))
        for j in range(2, MAXT):
            link(STT(qk, pk, float(j * P), qk, ALU.is_ge, ALU.add))
        link(STT(pk, qk, -float(P), pk, ALU.mult, ALU.add))
        token = rconst[:, 64:64 + NT]
        for c in range(2):
            link(TT(jq[:, c], over(r5.unsqueeze(1), NT, MAXT), over(qk[:, c].unsqueeze(2), NT, MAXT), ALU.is_equal))
            link(TT(jq[:, c], jq[:, c], over(token.unsqueeze(2), NT, MAXT), ALU.mult))
            for t in range(NT):
                link(TT(vhot[:, c, t], over(picks[:, c, t].unsqueeze(2), NE, MAXT),
                        over(jq[:, c, t].unsqueeze(1), NE, MAXT), ALU.mult))
                link(TS(phot[:, c, t, :], iota_row, pk[:, c, t:t + 1], None, ALU.is_equal), "rt_v")
        dve.wait_ge(S["idx_done"], 1)
        link(CP(idx_i, ps[:, 6, 0:NE * MAXT]), "route_ready")
        dve.wait_ge(S["rt_exp"], 1)
        w12 = rt(2, NT)
        link(dve.tensor_reduce(pg, rt_e, AX_X, ALU.add))
        link(TS(w12[:, 0], rt_d, 1.0, None, ALU.add))
        link(TT(w12[:, 0], w12[:, 0], pg, ALU.mult))
        link(dve.reciprocal(w12[:, 0], w12[:, 0]))
        link(TT(w12[:, 1], w12[:, 0], rt_d, ALU.mult))

        def x_half(i):
            dve.wait_ge(S["xt_t"], i + 1)
            dve.tensor_copy(xT[:, 4:8, :], ps[:, 1, :].rearrange("p (k t) -> p k t", t=P)).then_inc(S["xT_d"], 1)

        start_at_one(dve, "act_ready", "xT_d", "aT_d", "y_d")
        x_half(1)
        with dve.Fori(0, NE) as e:
            nt = dve.value_load(tiles_i[0:1, bass.ds(e, 1)], min_val=1, max_val=MAXT)
            first = dve.value_load(tiles_i[0:1, bass.ds(17 + e, 1)], min_val=1, max_val=TILES)
            with dve.Fori(0, nt) as j:
                i = first + j
                dve.wait_ge(S["up_mm"], i + 1)
                dve.wait_ge(S["silu_ready"], i + 1)
                dve.wait_ge(S["at_t"], i)
                dve.tensor_tensor(uact, ps[:, 3, :], gact, ALU.mult).then_inc(S["act_ready"], 1)
                x_half(i + 1)
                dve.wait_ge(S["at_t"], i + 1)
                dve.tensor_copy(aT[:, 2:4, :], ps[:, 7, 0:2 * P].rearrange("p (k t) -> p k t", t=P))\
                    .then_inc(S["aT_d"], 1)
                dve.wait_ge(S["down1"], i + 1)
                dve.wait_ge(S["y_stored"], 16 * i)
                dve.tensor_copy(ysb[:, CH:D], ps[:, 6, :]).then_inc(S["y_d"], 1)

        dve.wait_ge(S["ld_gr2"], 32)

        def weigh(t):
            dve.wait_ge(comb_gather[t], 32)
            y0, y1 = ypair[t][:, 0, :], ypair[t][:, 1, :]
            link(TS(y0, y0, w12[:, 0, t:t + 1], None, ALU.mult))
            link(STT(y0, y1, w12[:, 1, t:t + 1], y0, ALU.mult, ALU.add), "comb_v")

        weigh(0)
        for t in range(NT):
            if t + 1 < NT:
                weigh(t + 1)
            y0 = ypair[t][:, 0, :]
            dve.wait_ge(S["comb_rs"], t + 1)
            s = st1[:, 60 + t:61 + t]
            link(dve.reciprocal(s, s))
            link(STT(y0, y0, s, gr2[:, min(t, 1), :], ALU.mult, ALU.mult))
            link(TT(fin[t], y0, x2[:, t, :], ALU.add), "fin_ready")

    @block.tensor
    def _(pe):
        M = pe.matmul

        pe.wait_ge(S["ld_ident"], 16)
        pe.wait_ge(S["ld_rows"], 96)
        pe.transpose(ps[:, 0, 0:120], rows1, ident[0:120, 0:120]).then_inc(S["setup_t"], 1)
        pe.transpose(ps[:, 7, 0:16], rows2, ident[0:16, 0:16]).then_inc(S["setup_t"], 1)
        pe.wait_ge(S["ld_mlp"], 80)
        for layer, (w, x) in enumerate(((w1sb, feat), (w2sb, hid1))):
            if layer:
                pe.wait_ge(S["hid_ready"], 1)
            M(ps[0:FH, 1 + 2 * layer, :], w, x[:, CTX:TOK], start=True, stop=True)
            M(ps[0:FH, 2 + 2 * layer, 0:CTX], w, x[:, 0:CTX], start=True, stop=True).then_inc(S["mlp_done"], 1)
        pe.wait_ge(S["hid_ready"], 2)
        pe.wait_ge(S["ones_ready"], 4)
        pe.wait_ge(S["ld_w3"], 64)
        pe.wait_ge(S["cols_ready"], 1)
        pe.wait_ge(S["cvec_ready"], 1)

        def wait_chunk(n):
            pe.wait_ge(ring_full[n % 3], 16 * (n // 3 + 1))
            return slot[n % 3]

        def ada_chunk(n):
            w = wait_chunk(ADA_AT[n])
            bank = 0 if n < 4 else 7
            for q in range(NB):
                col = 2 * (n * NB + q)
                for k in range(KD):
                    mm = M(ps[:, bank, col:col + 2], w[:, k, q * P:(q + 1) * P], cvec[:, :, k],
                           start=k == 0, stop=k == KD - 1)
            mm.then_inc(S["chunk_used"], 1)

        def filter_bank(n):
            if n >= 4:
                pe.wait_ge(S["filt_read"], n - 3)
            return 1 + n % 4

        for o in range(ORD):
            for w in range(10):
                t, s, n = w // 2, w % 2, 22 * o + w
                b, c = filter_bank(n), (2 * o + s) * MW
                M(ps[:, b, :], hid2[:, t * P:(t + 1) * P], w3e[:, c:c + MW], start=True, stop=True)\
                    .then_inc(S["filt_done"], 1)
                if o and w == 5:
                    ada_chunk(3)
            ada_chunk(4 * o)
            pe.wait_ge(S["acc_done"], 10 * o + 10)
            if o:
                pe.wait_ge(S["norm_sqrt"], o)
            M(ps[:, 5, :], ones, sq_l, start=True, stop=True)
            M(ps[:, 6, :], ones, sq_c, start=True, stop=True).then_inc(S["norm_done"], 1)
            ada_chunk(4 * o + 1)
            pe.wait_ge(S["ab_ready"], o + 1)
            pe.wait_ge(S["ld_dft"], 96)
            for g in range(12):
                n = 22 * o + 10 + g
                b = filter_bank(n)
                if g in (2, 11):
                    if g == 2:
                        for tb in range(LT):
                            mm = M(ps[0:1, b, :], sin_l[:, tb, 0:1], ab[:, 0, 1 + tb, :], start=tb == 0, stop=tb == LT - 1)
                    else:
                        mm = M(ps[0:1, b, :], sin_c[:, 0:1], ab[:, 0, 0, :], start=True, stop=True)
                elif g >= 9:
                    mm = M(ps[:, b, :], (cos_c, sin_c)[g - 9], ab[:, g - 9, 0, :], start=True, stop=True)
                else:
                    q = g if g < 2 else g - 1
                    f, table = q // 2, (cos_l, sin_l)[q % 2]
                    for tb in range(LT):
                        mm = M(ps[:, b, :], table[:, tb, f * P:(f + 1) * P], ab[:, q % 2, 1 + tb, :],
                               start=tb == 0, stop=tb == LT - 1)
                mm.then_inc(S["filt_done"], 1)
                if g == (5 if o else 8):
                    ada_chunk(4 * o + 2)
        ada_chunk(7)

        pe.wait_ge(S["filt_read"], 44)
        pe.wait_ge(S["xn_ready"], NT)
        for n in range(10):
            b = 1 + n % 4
            if n >= 4:
                pe.wait_ge(S["xt_d" if n % 2 else "xt_a"], (n - 4) // 2 + 1)
            for q in range(4):
                t, k = (0, 4 * n + q) if n < 2 else (1 + q, n - 2)
                mm = pe.transpose(ps[:, b, q * P:(q + 1) * P], x_raw[:, t, k * P:(k + 1) * P], ident)
            mm.then_inc(S["xt_done"], 1)
        pe.wait_ge(S["xt_a"], 5)
        pe.wait_ge(S["xt_d"], 5)

        def channel_groups(w, blk, b, done, used=None):
            for k in range(KD):
                lhs = w[:, k, blk * P:(blk + 1) * P]
                M(ps[:, b, :], lhs, hT[:, k, CTX:TOK], start=k == 0, stop=k == KD - 1)
                mm = M(ps[:, b + 1, 0:CTX], lhs, hT[:, k, 0:CTX], start=k == 0, stop=k == KD - 1)
            mm.then_inc(S[done], 1)

        def to_tokens(n):
            pe.wait_ge(S["conv_d"], n + 1)
            if n >= 1:
                pe.wait_ge(S["tp_read"], n)
            u = ubuf[:, n % 2, :]
            for t in range(LT):
                pe.transpose(ps[:, 5, t * P:(t + 1) * P], u[:, (1 + t) * P:(2 + t) * P], ident)
            pe.transpose(ps[:, 6, 0:P], u[:, 0:CTX], ident).then_inc(S["tp_done"], 1)

        for n in range(12):
            w = wait_chunk(HY_AT[n // 4])
            if n >= 2:
                pe.wait_ge(S["conv_d"], n - 1)
            channel_groups(w, n % 4, 1 + 2 * (n % 2), "hy_done")
            if 1 <= n <= 8:
                to_tokens(n - 1)
            if n % 4 == 3:
                M(ps[0:2, 0, 510:512], w[:, 0, 0:2], cvec[:, :, 0], start=True, stop=True)\
                    .then_inc(S["chunk_used"], 1)
                ada_chunk(8 + n // 4)
        ada_chunk(11)

        def forward(o):
            z = part0 if o else part2
            for g in range(10):
                if o or g:
                    if 10 * o + g >= 4:
                        pe.wait_ge(S["fw_read"], 10 * o + g - 3)
                b = 1 + g % 4
                if g < 8:
                    f, table = g // 2, (cos_l, sin_l)[g % 2]
                    for tb in range(LT):
                        mm = M(ps[:, b, :], table[:, tb, f * P:(f + 1) * P], z[:, 1 + tb, :],
                               start=tb == 0, stop=tb == LT - 1)
                else:
                    mm = M(ps[:, b, :], (cos_c, sin_c)[g - 8], z[:, 0, :], start=True, stop=True)
                mm.then_inc(S["fw_done"], 1)

        def inverse_bank(n):
            if n >= 2:
                pe.wait_ge(S["iv_read"], n - 1)
            return 5 + n % 2

        pe.wait_ge(S["conv_d"], 12)
        pe.wait_ge(S["tp_read"], 8)
        forward(0)
        pe.wait_ge(S["mul_done"], 4)
        for t in range(NT):
            b = inverse_bank(t)
            if t < LT:
                for f in range(LT):
                    M(ps[:, b, :], cos_l[:, f, t * P:(t + 1) * P], spec_x[:, 0, f, :], start=f == 0, stop=False)
                    mm = M(ps[:, b, :], sint_l[:, f, t * P:(t + 1) * P], spec_x[:, 1, f, :], start=False, stop=f == LT - 1)
            else:
                pe.wait_ge(S["mul_done"], 5)
                M(ps[:, b, :], cos_c, spec_xc[:, 0, :], start=True, stop=False)
                mm = M(ps[:, b, :], sint_c, spec_xc[:, 1, :], start=False, stop=True)
            mm.then_inc(S["iv_done"], 1)
        pe.wait_ge(S["modB_ready"], 1)
        pe.transpose(ps[0:64, 0, 0:P], pack.rearrange("p v g k -> p (v g k)"), ident).then_inc(S["pack_t"], 1)

        def project_qk(which):
            w = wait_chunk(CHUNK_Q + which)
            pe.wait_ge(S["fw_read"], 10 + 10 * which)
            for n in range(NB):
                if n >= 2:
                    pe.wait_ge(S["qk_read"], NB * which + n - 1)
                channel_groups(w, n, 1 + 2 * (n % 2), "qk_done")
            M(ps[0:2, 0, 510:512], w[:, 0, 0:2], cvec[:, :, 0], start=True, stop=True).then_inc(S["chunk_used"], 1)

        pe.wait_ge(S["packT_ready"], 1)
        project_qk(0)
        pe.wait_ge(S["qk_read"], NB)
        pe.wait_ge(S["iv_read"], NT)
        forward(1)
        project_qk(1)
        pe.wait_ge(S["mul_done"], 10)
        for n in range(5):
            b = inverse_bank(NT + n)
            if n < NB:
                for f in range(LT):
                    M(ps[:, b, :], spec_x[:, 0, f, n * P:(n + 1) * P], cos_l[:, f, :], start=f == 0, stop=False)
                    mm = M(ps[:, b, :], spec_x[:, 1, f, n * P:(n + 1) * P], sint_l[:, f, :], start=False, stop=f == LT - 1)
            else:
                for c in range(NB):
                    M(ps[:, b, c * P:(c + 1) * P], spec_xc[:, 0, c * P:(c + 1) * P], cos_c, start=True, stop=False)
                    mm = M(ps[:, b, c * P:(c + 1) * P], spec_xc[:, 1, c * P:(c + 1) * P], sint_c, start=False, stop=True)
            mm.then_inc(S["iv_done"], 1)

        pe.wait_ge(S["ld_gate"], 112)
        for t in range(NT):
            for k in range(KD):
                mm = M(ps[:, 7, 16 * t:16 * t + 16], hT[:, k, t * P:(t + 1) * P], wgate[:, k, :],
                       start=k == 0, stop=k == KD - 1)
        mm.then_inc(S["gate_done"], 1)
        pe.wait_ge(S["qk_read"], 2 * NB)
        for t in range(NT):
            if t >= 4:
                pe.wait_ge(S["kt_read"], t - 3)
            for h in range(H):
                mm = pe.transpose(ps[:, 1 + t % 4, h * P:(h + 1) * P], kT[:, h, t * P:(t + 1) * P], ident)
            mm.then_inc(S["kt_done"], 1)
        pe.wait_ge(S["gate_read"], 1)
        pe.wait_ge(S["iv_read"], 10)
        for i in range(2):
            for t in range(NT):
                out = ps[0:ROWS, 0, i * P:(i + 1) * P] if t == 0 else ps[0:ROWS, 5 + i, (t - 1) * P:t * P]
                mm = pe.transpose(out, gpad[:, t, i, :], ident)
        mm.then_inc(S["gt_done"], 1)
        pe.wait_ge(S["kt_read"], NT)

        def token_group(n):
            chunk = CHUNK_Q + 2 + n // NT
            w, t = wait_chunk(chunk), n % NT
            if n >= 4:
                pe.wait_ge(S["vo_read"], n - 3)
            for k in range(KD):
                mm = M(ps[:, 1 + n % 4, :], hT[:, k, t * P:(t + 1) * P], w[:, k, :], start=k == 0, stop=k == KD - 1)
            mm.then_inc(S["vo_done"], 1)
            if t == NT - 1:
                M(ps[0:2, 0, 510:512], w[:, 0, 0:2], cvec[:, :, 0], start=True, stop=True).then_inc(S["chunk_used"], 1)

        for n in range(NT):
            token_group(n)
        pe.wait_ge(S["qrow_ready"], 1)
        pe.wait_ge(S["gt_read"], 1)
        for n, (t0, t1) in enumerate(((0, 3), (3, 5))):
            for t in range(t0, t1):
                for q in range(4):
                    c = ((t - t0) * 4 + q) * ROWS
                    mm = pe.transpose(ps[:, 5 + n, c:c + ROWS], g_q[:, q, t * P:(t + 1) * P], ident[0:ROWS, 0:ROWS])
            mm.then_inc(S["qc_done"], 1)
        pe.wait_ge(S["ld_late"], 16)
        for u in range(UNITS):
            mm = M(ps[:, 7, u * NT:(u + 1) * NT], sel[:, u, :], dec, start=True, stop=True)
        mm.then_inc(S["dec_done"], 1)
        for n in range(NT, 2 * NT):
            token_group(n)
        pe.wait_ge(S["qc_read"], 3)
        pe.wait_ge(S["vo_read"], 2 * NT)
        pe.wait_ge(S["vones"], 1)
        pe.wait_ge(S["ld_state"], 32)

        def broadcast_m(i):
            d, t = steps[i]
            if i:
                pe.wait_ge(S["e_ready"], i)
            for h in range(H):
                mm = M(ps[:, 0, h * P:(h + 1) * P], sel[:, H * d + h, :], g_nm[:, t * P:(t + 1) * P],
                       start=True, stop=True)
            mm.then_inc(S["bc_done"], 1)

        def scores(i):
            d, t = steps[i]
            if i:
                pe.wait_ge(S["p_ready"], i)
            for h in range(H):
                mm = M(ps[:, 1, h * P:(h + 1) * P], kT[:, h, t * P:(t + 1) * P], qT[:, h, t * P:(t + 1) * P],
                       start=True, stop=True)
            mm.then_inc(S["s_done"], 1)

        broadcast_m(0)
        scores(0)
        for i in range(NSTEP):
            d, t = steps[i]
            if i + 1 < NSTEP:
                broadcast_m(i + 1)
            if t:
                if i >= 4:
                    pe.wait_ge(S["st_ready"], i - 1)
                if i >= 3:
                    pe.wait_ge(S["inter_read"], i - 2)
                for h in range(H):
                    b, c = half4(h)
                    mm = M(ps[:, 4 + b, c:c + DH + 1], qT[:, h, t * P:(t + 1) * P], c_lat[:, d, h, :],
                           start=True, stop=True)
                mm.then_inc(S["inter_done"], 1)
            pe.wait_ge(S["p_ready"], i + 1)
            if i:
                pe.wait_ge(S["num_ready"], i)
            for h in range(H):
                b, c = half4(h)
                mm = M(ps[:, 2 + b, c:c + DH + 1], pbuf[:, i % 2, h, :], v_aug[:, t, h, :], start=True, stop=True)
            mm.then_inc(S["intra_done"], 1)
            if i + 1 < NSTEP:
                scores(i + 1)
            if i < LAST_UPD:
                pe.wait_ge(S["kw_ready"], i + 1)
                if i:
                    pe.wait_ge(S["st_ready"], i)
                for h in range(H):
                    b, c = half4(h)
                    mm = M(ps[:, 6 + b, c:c + DH + 1], kw[:, i % 2, h, :], v_aug[:, t, h, :], start=True, stop=True)
                mm.then_inc(S["upd_done"], 1)

        def turn_heads(t):
            pe.wait_ge(S["yml_ready"], t + 1)
            if t:
                pe.wait_ge(S["yt_read"], t)
            for h in range(H):
                mm = pe.transpose(ps[:, 0, h * P:(h + 1) * P], hbuf[:, t % 2, h, :], ident)
            mm.then_inc(S["yt_done"], 1)

        def out_project(t):
            pe.wait_ge(S["yt_read"], t + 1)
            if t >= 2:
                pe.wait_ge(S["x2_sq"], t - 1)
            for c in range(2):
                w = wait_chunk(CHUNK_OUT + c)
                for k in range(2 * NB):
                    src = ymlT if k < NB else part1t
                    mm = M(ps[:, 1 + 2 * (t % 2) + c, :], src[:, k % NB, t * P:(t + 1) * P], w[:, k, :],
                           start=k == 0, stop=k == 2 * NB - 1)
            mm.then_inc(S["wo_done"], 1)

        def turn_h2(t):
            pe.wait_ge(S["h2_ready"], t + 1)
            if t:
                pe.wait_ge(S["h2t_read"], t)
            for k in range(KD):
                mm = pe.transpose(ps[:, 5 + k // 4, (k % 4) * P:(k % 4 + 1) * P], h2buf[:, t % 2, k * P:(k + 1) * P], ident)
            mm.then_inc(S["h2t_done"], 1)

        def logits(t):
            pe.wait_ge(S["h2t_read"], t + 1)
            for k in range(KD):
                mm = M(ps[:, 7, 20 * t:20 * t + 20], h2T[:, t % 2, k, :], wrt[:, k, :], start=k == 0, stop=k == KD - 1)
            mm.then_inc(S["lg_done"], 1)

        pe.wait_ge(S["num_ready"], NSTEP)
        pe.wait_ge(S["st_ready"], LAST_UPD)
        pe.wait_ge(S["ld_route"], 80)
        turn_heads(0)
        for t in range(NT):
            out_project(t)
            if t + 1 < NT:
                turn_heads(t + 1)
            if t == NT - 1:
                for c in range(2):
                    M(ps[0:2, 0, 510:512], slot[(CHUNK_OUT + c) % 3][:, 0, 0:2], cvec[:, :, 0], start=True, stop=True)\
                        .then_inc(S["chunk_used"], 1)
            if t:
                turn_h2(t - 1)
            if t >= 2:
                logits(t - 2)
        logits(NT - 2)
        turn_h2(NT - 1)
        logits(NT - 1)

        pe.wait_ge(S["rt_v"], 1)
        flat = used.rearrange("p t e -> p (t e)")
        M(ps[:, 5, 0:NT * NE], tri, flat, start=True, stop=True)
        M(ps[:, 6, 0:NT * NE], ones, flat, start=True, stop=True).then_inc(S["pos_done"], 1)
        for n in range(2 * NT):
            pe.wait_ge(S["rt_v"], n + 2)
            c, t = n // NT, n % NT
            mm = M(ps[:, 6, 0:NE * MAXT], phot[:, c, t, :], vhot[:, c, t].rearrange("p e j -> p (e j)"),
                   start=n == 0, stop=n == 2 * NT - 1)
        mm.then_inc(S["idx_done"], 1)
        pe.wait_ge(S["route_ready"], 1)

        def turn_rows(i):
            pe.wait_ge(S["gather"], 16 * i)
            pe.wait_ge(S["xT_a"], i)
            pe.wait_ge(S["xT_d"], i)
            for k in range(KD):
                mm = pe.transpose(ps[:, k // 4, (k % 4) * P:(k % 4 + 1) * P], xrows[:, k * P:(k + 1) * P], ident)
            mm.then_inc(S["xt_t"], 1)

        start_at_one(pe, "gate_mm", "up_mm", "down0", "down1", "xt_t", "at_t")
        turn_rows(1)
        with pe.Fori(0, NE // 2) as pair:
            for half in range(2):
                e = 2 * pair + half
                nt = pe.value_load(tiles_i[0:1, bass.ds(e, 1)], min_val=1, max_val=MAXT)
                first = pe.value_load(tiles_i[0:1, bass.ds(17 + e, 1)], min_val=1, max_val=TILES)
                wg, wu, wd = slot[3 * half], slot[3 * half + 1], down_slot[3 * half + 2]
                full = w_full[half]
                with pe.Fori(0, nt) as j:
                    i = first + j
                    pe.wait_ge(S["xT_a"], i + 1)
                    pe.wait_ge(S["xT_d"], i + 1)
                    pe.wait_ge(full[0], 16 * pair + 16)
                    pe.wait_ge(S["silu_ready"], i)
                    for k in range(KD):
                        mm = M(ps[:, 2, :], xT[:, k, :], wg[:, k, :], start=k == 0, stop=k == KD - 1)
                    mm.then_inc(S["gate_mm"], 1)
                    pe.wait_ge(full[1], 16 * pair + 16)
                    pe.wait_ge(S["act_ready"], i)
                    for k in range(KD):
                        mm = M(ps[:, 3, :], xT[:, k, :], wu[:, k, :], start=k == 0, stop=k == KD - 1)
                    mm.then_inc(S["up_mm"], 1)
                    turn_rows(i + 1)
                    pe.wait_ge(S["act_ready"], i + 1)
                    pe.wait_ge(S["aT_a"], i)
                    pe.wait_ge(S["aT_d"], i)
                    for k in range(FF // P):
                        mm = pe.transpose(ps[:, (4, 7)[k // 2], (k % 2) * P:(k % 2 + 1) * P],
                                          uact[:, k * P:(k + 1) * P], ident)
                    mm.then_inc(S["at_t"], 1)
                    pe.wait_ge(full[2], 16 * pair + 16)
                    pe.wait_ge(S["aT_a"], i + 1)
                    pe.wait_ge(S["aT_d"], i + 1)
                    pe.wait_ge(S["y_a"], i)
                    pe.wait_ge(S["y_d"], i)
                    for c in range(2):
                        for k in range(FF // P):
                            mm = M(ps[:, 5 + c, :], aT[:, k, :], wd[:, k, c * CH:(c + 1) * CH],
                                   start=k == 0, stop=k == FF // P - 1)
                        mm.then_inc(S[("down0", "down1")[c]], 1)


_INS = ["x_prompt", "x_sample", "state_C", "state_n", "state_m", "c", "c_ctx", "w_ada", "b_ada", "g_norm", "w_in",
        "ml_gate_bias", "ml_head_gain", "hy_conv_w", "hy_f_w1", "hy_f_b1", "hy_f_w2", "hy_f_b2", "hy_f_w3", "hy_f_b3",
        "hy_decay", "hy_bias", "w_out", "w_rc", "b_rc", "w_rf", "b_rf", "w_gate", "w_up", "w_down"]
_OUTS = [("out_p", (1, CTX, D)), ("out_s", (1, LAT, D)), ("out_C", (1, 1, 2, H, DH, DH)), ("out_n", (1, 1, 2, H, DH)),
         ("out_m", (1, 1, 2, H))]


def kernel(**inputs):
    import concourse.bacc as bacc
    from concourse.bass_utils import run_bass_kernel_spmd

    nc = bacc.Bacc("TRN2", target_bir_lowering=False, num_devices=1)
    arrays, aps = {}, {}
    tables = shape_constants()
    for name in _INS + CONST_NAMES:
        x = np.ascontiguousarray(inputs[name] if name in inputs else tables[name])
        arrays["in_" + name] = x
        aps[name] = nc.dram_tensor("in_" + name, x.shape, F32, kind="ExternalInput").ap()
    for name, shape in _OUTS:
        aps[name] = nc.dram_tensor(name, shape, F32, kind="ExternalOutput").ap()
    build(nc, aps)
    got = run_bass_kernel_spmd(nc, [arrays], core_ids=[0]).results[0]
    return tuple(got[name] for name, _ in _OUTS)
```
